# Optimizing a Trainium2 kernel written in Bass

```python
import jax, jax.numpy as jnp
from jax import lax
import numpy as np

D_MODEL = 1024
BATCH = 1
SEQ = 512
DEPTH = 2

HEAD_DIM = 64
ATTN_HEADS = (D_MODEL // 2) // HEAD_DIM
ATTN_KV_HEADS = ATTN_HEADS // 4
WINDOW = 128
ATTN_BLOCK = 128
ROPE_THETA = 10000.0
CONV_CH = D_MODEL // 2
CONV_WIDTH = 3
Q_W = ATTN_HEADS * HEAD_DIM
KV_W = ATTN_KV_HEADS * HEAD_DIM
EVEN_IN_W = Q_W + 2 * KV_W + 3 * CONV_CH
EVEN_MIX_W = Q_W + CONV_CH
DN_HEAD_DIM = 128
DN_HEADS = D_MODEL // DN_HEAD_DIM
DN_W = DN_HEADS * DN_HEAD_DIM
DN_CONV_WIDTH = 4
DN_CHUNK = 64
ODD_IN_W = 4 * DN_W + 2 * DN_HEADS
D_FF = -(-8 * D_MODEL // (3 * 256)) * 256
EPS = 1e-6
N_EVEN = (DEPTH + 1) // 2
N_ODD = DEPTH // 2

kernel_name = 'hybrid_swa_shortconv_gdn_block'

def rms_norm(x, g):
    xf = x.astype(jnp.float32)
    y = xf * lax.rsqrt(jnp.mean(xf * xf, axis=-1, keepdims=True) + EPS) * g.astype(jnp.float32)
    return y.astype(x.dtype)

def l2_norm(x):
    return x * lax.rsqrt(jnp.sum(x * x, axis=-1, keepdims=True) + EPS)

def rope_tables(seq_len):
    inv_freq = ROPE_THETA ** (-jnp.arange(0, HEAD_DIM, 2, dtype=jnp.float32) / HEAD_DIM)
    ang = jnp.arange(seq_len, dtype=jnp.float32)[:, None] * inv_freq[None, :]
    return jnp.cos(ang), jnp.sin(ang)

def apply_rope(x, cos, sin):
    xf = x.astype(jnp.float32)
    half = HEAD_DIM // 2
    x1, x2 = xf[..., :half], xf[..., half:]
    c, s = cos[None, :, None, :], sin[None, :, None, :]
    return jnp.concatenate([x1 * c - x2 * s, x2 * c + x1 * s], axis=-1).astype(x.dtype)

def causal_depthwise_conv(u, w):
    width, ch = w.shape
    return lax.conv_general_dilated(
        u, w[:, None, :].astype(u.dtype), window_strides=(1,), padding=[(width - 1, 0)],
        dimension_numbers=('NWC', 'WIO', 'NWC'), feature_group_count=ch)

def sliding_window_attention(q, k, v, sinks):
    bsz, t, h, d = q.shape
    kvh = k.shape[2]
    grp = h // kvh
    nb = t // ATTN_BLOCK
    qb = q.reshape(bsz, nb, ATTN_BLOCK, kvh, grp, d)

    def band(z):
        pad = jnp.zeros((bsz, ATTN_BLOCK, kvh, d), z.dtype)
        zp = jnp.concatenate([pad, z], axis=1).reshape(bsz, nb + 1, ATTN_BLOCK, kvh, d)
        return jnp.concatenate([zp[:, :-1], zp[:, 1:]], axis=2)

    kb, vb = band(k), band(v)
    s = jnp.einsum('bnqkgd,bnskd->bnkgqs', qb, kb,
                   preferred_element_type=jnp.float32) * (d ** -0.5)
    blk = jnp.arange(nb)[:, None] * ATTN_BLOCK
    q_pos = blk + jnp.arange(ATTN_BLOCK)[None, :]
    k_pos = blk - ATTN_BLOCK + jnp.arange(2 * ATTN_BLOCK)[None, :]
    diff = q_pos[:, :, None] - k_pos[:, None, :]
    valid = (diff >= 0) & (diff < WINDOW) & (k_pos[:, None, :] >= 0)
    s = jnp.where(valid[None, :, None, None], s, -jnp.inf)
    sink = jnp.broadcast_to(sinks.astype(jnp.float32).reshape(kvh, grp)[None, None, :, :, None, None],
                            s.shape[:-1] + (1,))
    p = jax.nn.softmax(jnp.concatenate([s, sink], axis=-1), axis=-1)[..., :-1]
    o = jnp.einsum('bnkgqs,bnskd->bnqkgd', p.astype(v.dtype), vb)
    return o.reshape(bsz, t, h * d)

def attn_conv_mixer(h, w_in, q_gain, k_gain, sinks, conv_w, w_out, cos, sin):
    bsz, t, _ = h.shape
    proj = h @ w_in
    q, k, v, gate_b, gate_c, xin = jnp.split(
        proj, np.cumsum([Q_W, KV_W, KV_W, CONV_CH, CONV_CH]).tolist(), axis=-1)
    q = apply_rope(rms_norm(q.reshape(bsz, t, ATTN_HEADS, HEAD_DIM), q_gain), cos, sin)
    k = apply_rope(rms_norm(k.reshape(bsz, t, ATTN_KV_HEADS, HEAD_DIM), k_gain), cos, sin)
    v = v.reshape(bsz, t, ATTN_KV_HEADS, HEAD_DIM)
    y_attn = sliding_window_attention(q, k, v, sinks)
    y_conv = gate_b * causal_depthwise_conv(gate_c * xin, conv_w)
    return jnp.concatenate([y_attn, y_conv], axis=-1) @ w_out

def chunk_gated_delta_rule(q, k, v, beta, g):
    bsz, t, h, dk = q.shape
    dv = v.shape[-1]
    n = t // DN_CHUNK

    def chunks(z):
        return z.reshape(bsz, n, DN_CHUNK, h, -1).transpose(0, 1, 3, 2, 4)

    q, k, v = chunks(q), chunks(k), chunks(v)
    beta = chunks(beta[..., None])[..., 0]
    gc = jnp.cumsum(chunks(g[..., None])[..., 0], axis=-1)
    idx = jnp.arange(DN_CHUNK)
    lower = idx[:, None] >= idx[None, :]
    strict = idx[:, None] > idx[None, :]
    gamma = jnp.exp(jnp.where(lower, gc[..., :, None] - gc[..., None, :], -jnp.inf))
    kb = k * beta[..., None]
    a_mat = jnp.where(strict, jnp.einsum('bnhcd,bnhsd->bnhcs', kb, k) * gamma, 0.0)
    m_mat = a_mat + jnp.eye(DN_CHUNK, dtype=a_mat.dtype)
    rhs = jnp.concatenate([v * beta[..., None], kb * jnp.exp(gc)[..., None]], axis=-1)
    sol = lax.linalg.triangular_solve(m_mat, rhs, left_side=True, lower=True, unit_diagonal=True)
    u, w = sol[..., :dv], sol[..., dv:]
    attn_intra = jnp.einsum('bnhcd,bnhsd->bnhcs', q, k) * gamma
    q_dec = q * jnp.exp(gc)[..., None]
    k_dec = k * jnp.exp(gc[..., -1:] - gc)[..., None]
    chunk_decay = jnp.exp(gc[..., -1])

    def step(state, xs):
        qd, kd, u_i, w_i, a_i, dec = xs
        v_new = u_i - jnp.einsum('bhcd,bhde->bhce', w_i, state)
        o = jnp.einsum('bhcd,bhde->bhce', qd, state) + jnp.einsum('bhcs,bhse->bhce', a_i, v_new)
        state = state * dec[..., None, None] + jnp.einsum('bhcd,bhce->bhde', kd, v_new)
        return state, o

    xs = tuple(jnp.moveaxis(z, 1, 0) for z in (q_dec, k_dec, u, w, attn_intra, chunk_decay))
    s0 = jnp.zeros((bsz, h, dk, dv), jnp.float32)
    _, o = lax.scan(step, s0, xs)
    return o.transpose(1, 0, 3, 2, 4).reshape(bsz, t, h, dv)

def gated_deltanet_mixer(h, w_in, conv_w, a_log, dt_bias, o_gain, w_out):
    bsz, t, _ = h.shape
    proj = h @ w_in
    qkv, z, b_logit, a_logit = jnp.split(
        proj, [3 * DN_W, 4 * DN_W, 4 * DN_W + DN_HEADS], axis=-1)
    qkv = jax.nn.silu(causal_depthwise_conv(qkv, conv_w)).astype(jnp.float32)
    q, k, v = jnp.split(qkv, 3, axis=-1)
    q = l2_norm(q.reshape(bsz, t, DN_HEADS, DN_HEAD_DIM)) * (DN_HEAD_DIM ** -0.5)
    k = l2_norm(k.reshape(bsz, t, DN_HEADS, DN_HEAD_DIM))
    v = v.reshape(bsz, t, DN_HEADS, DN_HEAD_DIM)
    beta = jax.nn.sigmoid(b_logit.astype(jnp.float32))
    g = -jnp.exp(a_log.astype(jnp.float32)) * jax.nn.softplus(
        a_logit.astype(jnp.float32) + dt_bias.astype(jnp.float32))
    o = chunk_gated_delta_rule(q, k, v, beta, g)
    zf = z.reshape(bsz, t, DN_HEADS, DN_HEAD_DIM).astype(jnp.float32)
    o = rms_norm(o, o_gain) * jax.nn.silu(zf)
    return o.reshape(bsz, t, DN_W).astype(h.dtype) @ w_out

def swiglu_ffn(h, w_gate_up, w_down):
    gate, up = jnp.split(h @ w_gate_up, 2, axis=-1)
    return (jax.nn.silu(gate) * up) @ w_down

def setup_inputs(seed: int = 0) -> dict:
    key = jax.random.key(seed)
    ks = jax.random.split(key, 20)
    nrm = lambda k_, shape, scale: jax.random.normal(k_, shape, jnp.float32) * scale
    dt = jnp.exp(jax.random.uniform(ks[12], (N_ODD, DN_HEADS), jnp.float32,
                                    np.log(1e-3), np.log(1e-1)))
    return {
        'x': nrm(ks[0], (BATCH, SEQ, D_MODEL), 1.0),
        'even_norm': 1.0 + nrm(ks[1], (N_EVEN, D_MODEL), 0.02),
        'even_w_in': nrm(ks[2], (N_EVEN, D_MODEL, EVEN_IN_W), D_MODEL ** -0.5),
        'even_q_gain': 1.0 + nrm(ks[3], (N_EVEN, HEAD_DIM), 0.02),
        'even_k_gain': 1.0 + nrm(ks[4], (N_EVEN, HEAD_DIM), 0.02),
        'even_sinks': nrm(ks[5], (N_EVEN, ATTN_HEADS), 0.5),
        'even_conv_w': nrm(ks[6], (N_EVEN, CONV_WIDTH, CONV_CH), CONV_WIDTH ** -0.5),
        'even_w_out': nrm(ks[7], (N_EVEN, EVEN_MIX_W, D_MODEL), EVEN_MIX_W ** -0.5),
        'odd_norm': 1.0 + nrm(ks[8], (N_ODD, D_MODEL), 0.02),
        'odd_w_in': nrm(ks[9], (N_ODD, D_MODEL, ODD_IN_W), D_MODEL ** -0.5),
        'odd_conv_w': nrm(ks[10], (N_ODD, DN_CONV_WIDTH, 3 * DN_W), DN_CONV_WIDTH ** -0.5),
        'odd_a_log': jnp.log(jax.random.uniform(ks[11], (N_ODD, DN_HEADS), jnp.float32, 1.0, 16.0)),
        'odd_dt_bias': dt + jnp.log(-jnp.expm1(-dt)),
        'odd_o_gain': 1.0 + nrm(ks[13], (N_ODD, DN_HEAD_DIM), 0.02),
        'odd_w_out': nrm(ks[14], (N_ODD, DN_W, D_MODEL), DN_W ** -0.5),
        'ffn_norm': 1.0 + nrm(ks[15], (DEPTH, D_MODEL), 0.02),
        'ffn_w_gate_up': nrm(ks[16], (DEPTH, D_MODEL, 2 * D_FF), D_MODEL ** -0.5),
        'ffn_w_down': nrm(ks[17], (DEPTH, D_FF, D_MODEL), D_FF ** -0.5),
    }

def reference(x, even_norm, even_w_in, even_q_gain, even_k_gain, even_sinks, even_conv_w,
              even_w_out, odd_norm, odd_w_in, odd_conv_w, odd_a_log, odd_dt_bias, odd_o_gain,
              odd_w_out, ffn_norm, ffn_w_gate_up, ffn_w_down):
    cos, sin = rope_tables(x.shape[1])
    for layer in range(DEPTH):
        i = layer // 2
        if layer % 2 == 0:
            x = x + attn_conv_mixer(rms_norm(x, even_norm[i]), even_w_in[i], even_q_gain[i],
                                    even_k_gain[i], even_sinks[i], even_conv_w[i],
                                    even_w_out[i], cos, sin)
        else:
            x = x + gated_deltanet_mixer(rms_norm(x, odd_norm[i]), odd_w_in[i], odd_conv_w[i],
                                         odd_a_log[i], odd_dt_bias[i], odd_o_gain[i],
                                         odd_w_out[i])
        x = x + swiglu_ffn(rms_norm(x, ffn_norm[layer]), ffn_w_gate_up[layer], ffn_w_down[layer])
    return x


_drawn_inputs = setup_inputs


def setup_inputs(seed=0):
    import zlib

    import numpy as np

    out = dict(_drawn_inputs(seed))
    spreads = {}
    factors = {'even_q_gain': 8.0,
     'even_k_gain': 8.0,
     'even_sinks': 64.0,
     'odd_norm': 4.319,
     'odd_o_gain': 17.691,
     'ffn_norm': 2.963}
    for name, (base, spread) in spreads.items():
        noise = np.random.default_rng([zlib.crc32(name.encode()), seed]).standard_normal(out[name].shape)
        drawn = base * np.exp(spread * noise) if base else spread * noise
        out[name] = __import__('jax').numpy.asarray(drawn.astype(out[name].dtype))
    for name, factor in factors.items():
        out[name] = (out[name] * factor).astype(out[name].dtype)
    return out
```

```python
from contextlib import ExitStack

import numpy as np

import concourse.bass as bass
from concourse import mybir

F32 = mybir.dt.float32
F32R = mybir.dt.float32r
U32 = mybir.dt.uint32
ALU = mybir.AluOpType
ACT = mybir.ActivationFunctionType
AX = mybir.AxisListType

P = 128
T = 512
D = 1024
KT = D // P
HEAD = 64
NB = T // P
FF = 2816
FT = FF // P
FH = FT // 2
UW = P
DN_HEADS = 8
EPS = 1e-6
RING = 4
SLOT = FH * UW
NEG = -1e30

IN0_UNITS, OUT_UNITS, GU_UNITS, DOWN_UNITS, IN1_UNITS = 18, 8, 44, 16, 32
U_IN0 = 0
U_OUT0 = U_IN0 + IN0_UNITS
U_GU0 = U_OUT0 + OUT_UNITS
U_DOWN0 = U_GU0 + GU_UNITS
U_IN1 = U_DOWN0 + DOWN_UNITS
U_OUT1 = U_IN1 + IN1_UNITS
U_GU1 = U_OUT1 + OUT_UNITS
U_DOWN1 = U_GU1 + GU_UNITS
U_END = U_DOWN1 + DOWN_UNITS
E_IN0 = 0
E_OUT0 = E_IN0 + 18
E_GU0 = E_OUT0 + 8
E_DOWN0 = E_GU0 + 44
E_IN1 = E_DOWN0 + 8
E_OUT1 = E_IN1 + 32
E_GU1 = E_OUT1 + 8
E_DOWN1 = E_GU1 + 44

K_ONES, K_EPS, K_N = 0, P, P + 1
C_ID, C_UP, C_LOW = 0, P, 2 * P
C0_HALF, C0_ROT, C0_SUP = 3 * P, 4 * P, 5 * P
C0_COS = 6 * P
C0_SIN = C0_COS + T
C0_NEG = C0_SIN + T
C0_N = C0_NEG + 1
C1_PAIR, C1_OFF, C1_DIAG = 3 * P, 4 * P, 10 * P
C1_N = 16 * P
R_GAIN = 0
R_QG = 32
R_KG = 33
R_SINK = 34
R_CONV0 = 42
R_ALOG = 54
R_DT = 62
R_OG = 70
R_HEAD = 71
R_BA = R_HEAD + 96
R_N = R_BA + 128
H_TAP, H_G, H_GC, H_BETA, H_NBETA, H_N = 0, 12, 16, 20, 24, 28


class Steps:

    def __init__(self, sem, names):
        self.sem = sem
        self.names = names.split()

    def after(self, n, step):
        return n * len(self.names) + self.names.index(step) + 1


def trunk(nc, xT, params, kept, consts0, consts1, w_in0, w_out0, w_gu0, w_down0, w_in1, w_out1, w_gu1, w_down1, outT):
    with ExitStack() as ctx:
        def sb(name, shape, dt=F32):
            return ctx.enter_context(nc.sbuf_tensor(name, shape, dt))

        def sem(name):
            return ctx.enter_context(nc.semaphore(name))

        x = sb("x", [P, KT, T])
        mov_hi = sb("mov_hi", [P, KT, T], F32R)
        mov_lo = sb("mov_lo", [P, KT, T], F32R)
        raw = sb("raw", [P, RING, SLOT])
        w_hi = sb("w_hi", [P, 2, SLOT], F32R)
        w_lo = sb("w_lo", [P, 2, SLOT], F32R)
        kpt = sb("kpt", [P, K_N])
        prm = sb("prm", [P, R_N])
        rstd = sb("rstd", [P, T])
        sq = sb("sq", [P, 2, T])
        sqsum = sb("sqsum", [P, T])

        l0 = ExitStack()

        def sb0(name, shape, dt=F32):
            return l0.enter_context(nc.sbuf_tensor(name, shape, dt))

        cst0 = sb0("cst0", [P, C0_N])
        qk = sb0("qk", [P, 5, T])
        vT = sb0("vT", [P, T])
        rstd2 = sb0("rstd2", [P, T])
        vtok = sb0("vtok", [P, NB, P])
        hsq = sb0("hsq", [P, 2, T])
        hrs = sb0("hrs", [P, 2, T])
        rope_c = sb0("rope_c", [P, 2, T])
        rope_s = sb0("rope_s", [P, T])
        gate_c = sb0("gate_c", [P, 2, T])
        cx = sb0("cx", [P, 2, T + 2])
        conv0 = sb0("conv0", [P, 2, T])
        prob = sb0("prob", [P, 2, 4, P])
        probT = sb0("probT", [P, 2, 2, 4, P])
        mx = sb0("mx", [P, 2, 4])
        nmx = sb0("nmx", [P, 2, 4])
        sgap = sb0("sgap", [P, 2, 4])
        esink = sb0("esink", [P, 2, 4])
        den = sb0("den", [P, 2, 4])
        den2 = sb0("den2", [P, 2, 4])
        rden = sb0("rden", [P, 2, 4])
        nsink = sb0("nsink", [P, 8])
        mix = sb0("mix", [P, KT, T])
        l0.close()
        lf = ExitStack()
        act_hi = lf.enter_context(nc.sbuf_tensor("act_hi", [P, FT, T], F32R))
        act_lo = lf.enter_context(nc.sbuf_tensor("act_lo", [P, FT, T], F32R))
        gs = lf.enter_context(nc.sbuf_tensor("gs", [P, 2, T], F32))
        us = lf.enter_context(nc.sbuf_tensor("us", [P, 2, T], F32))
        lf.close()
        cst1 = sb("cst1", [P, C1_N])
        u = sb("u", [P, 3, T + 3])
        qkv = sb("qkv", [P, 2, 3, T])
        nsq = sb("nsq", [P, 2, T])
        nrs = nsq
        eR = sb("eR", [P, T])
        gam = sb("gam", [P, NB, P])
        gamL = sb("gamL", [P, NB, P])
        gamU = gam
        kd = sb("kd", [P, 2, T])
        qd = sb("qd", [P, 2, T])
        attT = sb("attT", [P, 2, NB, P])
        kdec = sb("kdec", [P, 2, NB, P])
        bv = sb("bv", [P, 2, NB, P])
        nA = sb("nA", [P, NB, P])
        W = sb("W", [P, 2, 2, P])
        WT = sb("WT", [P, 2, P])
        M = sb("M", [P, 2, 2, P])
        MT = sb("MT", [P, 2, 2, P])
        R = sb("R", [P, 2, 2, P])
        V = sb("V", [P, 2, 2, P])
        Y = sb("Y", [P, 2, P])
        XT = sb("XT", [P, 2, NB, P])
        S = sb("S", [P, P])
        R1 = sb("R1", [P, P])
        vn = sb("vn", [P, P])
        hp = sb("hp", [P, 2, H_N])
        decb = sb("decb", [P, 2, NB])
        betab = sb("betab", [P, 2, NB])
        HP = sb("HP", [P, DN_HEADS, H_N])
        ors = sb("ors", [P, T])
        osq, og = sq[:, 0, :], sq[:, 1, :]
        dno = sb("dno", [P, KT, T])
        ba = gam[0:16].rearrange("p c n -> p (c n)")
        bt = sb("bt", [P, NB, 16])
        esum = sb("esum", [P, 8])
        sm = sb("sm", [P, 8, NB, 8])

        bank = [ctx.enter_context(nc.psum_tensor(f"bank{i}", [P, T], F32)) for i in range(8)]

        def c_(at, layer=0, n=P):
            return (cst0, cst1)[layer][:, at:at + n]

        ones, eps_col = kpt[:, K_ONES:K_ONES + P], kpt[:, K_EPS:K_EPS + 1]
        ident = [c_(C_ID, n) for n in range(2)]
        upper = [c_(C_UP, n) for n in range(2)]
        lower = [c_(C_LOW, n) for n in range(2)]

        def chunks(ap):
            return ap.rearrange("p (c n) -> p c n", n=P)

        def over_chunks(ap, n=NB):
            return ap.unsqueeze(1).to_broadcast([P, n, ap.shape[1]])

        def along(ap, n=P):
            return ap.unsqueeze(2).to_broadcast([P, ap.shape[1], n])

        x_loaded = [sem(f"x_loaded{i}") for i in range(4)]
        kept_loaded = sem("kept_loaded")
        cst_loaded = sem("cst_loaded")
        prm_loaded = sem("prm_loaded")
        unit_loaded = [sem(f"unit_loaded{i}") for i in range(RING)]
        w_hi_ready = sem("w_hi_ready")
        w_lo_ready = sem("w_lo_ready")
        hi_ready = sem("hi_ready")
        lo_ready = sem("lo_ready")
        passes = sem("passes")
        taken = sem("taken")
        squared = sem("squared")
        added = Steps(sem("added"), "zero t0 t1 t2 t3 t4 t5 t6 t7")
        norm_sum = sem("norm_sum")
        rstd_log = sem("rstd_log")
        rstd_ready = sem("rstd_ready")
        rstd2_ready = sem("rstd2_ready")
        out_done = sem("out_done")
        hd_sq = sem("hd_sq")
        hd_sum = sem("hd_sum")
        hd_norm = Steps(sem("hd_norm"), "log rsqrt")
        hd_gain = sem("hd_gain")
        hd_rot = sem("hd_rot")
        hd_cos = sem("hd_cos")
        hd_rope = Steps(sem("hd_rope"), "sin sum")
        v_turned = sem("v_turned")
        v_tok = sem("v_tok")
        nsink_ready = sem("nsink_ready")
        scored = sem("scored")
        sm_max = Steps(sem("sm_max"), "join max neg gap")
        sm_exp = Steps(sem("sm_exp"), "e0 e1 e2 e3 sink")
        sm_den = Steps(sem("sm_den"), "sum recip")
        sm_div = sem("sm_div")
        turned = sem("turned")
        sm_mask = Steps(sem("sm_mask"), "cur prev")
        pv_done = sem("pv_done")
        y_copied = sem("y_copied")
        cc_tap = sem("cc_tap")
        cc_vec = Steps(sem("cc_vec"), "tap1 tap2")
        cc_scale = sem("cc_scale")
        pad0 = sem("pad0")
        silu_g = sem("silu_g")
        gated = sem("gated")
        act_hi_ready = sem("act_hi_ready")
        act_lo_ready = sem("act_lo_ready")
        gt_x = sem("gt_x")
        gt_x_used = sem("gt_x_used")
        gt_pe = Steps(sem("gt_pe"), "turned cum")
        gt_vec = Steps(sem("gt_vec"), "scaled copied taps plus1 beta beta_h nbeta_h z nabs relu "
                                      "softplus g g_h gc_h")
        gt_act = Steps(sem("gt_act"), "ea ebeta eabs log")
        zeroed = sem("zeroed")
        fetched = sem("fetched")
        tap0 = Steps(sem("tap0"), "q k v")
        taps = Steps(sem("taps"), "q1 q2 q3 k1 k2 k3 v1 v2 v3")
        silu = Steps(sem("silu"), "z q k v")
        pr_pe = Steps(sem("pr_pe"), "sumq sumk rows gram turnA qk turnK turnV")
        pr_vec = Steps(sem("pr_vec"), "kn qn d0 d1 d2 d3 gap A0 A1 A2 A3 W WT m M R att kdec bv dec beta")
        pr_act = Steps(sem("pr_act"), "sqq sqk lnq rsq lnk rsk eR gam")
        pr_pool = Steps(sem("pr_pool"), "gamL gamU m MT V kd qd")
        iv_pe = Steps(sem("iv_pe"), "Y1 Z1 T1 Y2 Z2 T2 Y3 Z3 T3 Y4 Z4 T4 Y5 Z5 T5 Y6 Z6 T6")
        iv_vec = Steps(sem("iv_vec"), "Y1 M1 R1 T1 V1 Y2 M2 R2 T2 V2 Y3 M3 R3 T3 V3 Y4 M4 R4 T4 V4 "
                                      "Y5 M5 R5 T5 V5 Y6 M6 XB T6 XA")
        sc_pe = Steps(sem("sc_pe"), "v0 o0 k1 v1 o1 k2 v2 o2 k3 v3 o3 sum")
        sc_vec = Steps(sem("sc_vec"), "vn0 S0 r1 vn1 S1 r2 vn2 S2 r3 vn3 gain out")
        sc_act = Steps(sem("sc_act"), "sq log rs")

        block = ctx.enter_context(nc.Block())

        def step(eng, of, n, name):
            if not isinstance(n, int) or n >= 0:
                eng.wait_ge(of.sem, of.after(n, name))

        def many(eng, s, n):
            if not isinstance(n, int) or n > 0:
                eng.wait_ge(s, n)

        def pairs(ap):
            return ap.rearrange("p (q n) -> p q n", n=P)

        def flat(ap):
            return ap.rearrange("p c n -> p (c n)")

        @block.sync
        def _(sp):
            def load(unit0, rounds, src, kt):
                if not (isinstance(rounds, int) and unit0 + RING * rounds < RING):
                    sp.wait_ge(w_lo_ready, unit0 - RING + 1 + RING * rounds)
                slot = unit0 % RING
                sp.dma_start(raw[:, slot, 0:kt * UW], src).then_inc(unit_loaded[slot], 16)

            def phase(unit0, w, kt, rounds):
                with sp.Fori(0, rounds) as i:
                    for n in range(RING):
                        load(unit0 + n, i, w[4 * i + n], kt)

            for n in range(IN0_UNITS):
                load(U_IN0 + n, 0, w_in0[n], KT)
            phase(U_OUT0, w_out0, KT, 2)
            phase(U_GU0, w_gu0, KT, 11)
            phase(U_DOWN0, w_down0, FH, 4)
            phase(U_IN1, w_in1, KT, 8)
            phase(U_OUT1, w_out1, KT, 2)
            phase(U_GU1, w_gu1, KT, 11)
            phase(U_DOWN1, w_down1, FH, 4)

        @block.tensor
        def _(pe):
            def unit_ap(w, unit0):
                return w[:, unit0 % 2, :].rearrange("p (k n) -> p k n", n=UW)

            def hi_passes(dst, unit0, src_hi, src_lo, ks, first, each=None):
                w = unit_ap(w_hi, unit0)
                for n, k in enumerate(ks):
                    if each:
                        each(n)
                    pe.matmul(dst, w[:, k, :], src_hi[:, k, :], start=first and n == 0, stop=False)
                    pe.matmul(dst, w[:, k, :], src_lo[:, k, :], start=False, stop=False)

            def lo_passes(dst, unit0, src_hi, ks, last):
                w = unit_ap(w_lo, unit0)
                for n, k in enumerate(ks):
                    mm = pe.matmul(dst, w[:, k, :], src_hi[:, k, :], start=False,
                                   stop=last and n == len(ks) - 1)
                return mm

            def project(dst, unit0, rounds, ks=range(KT), src_hi=mov_hi, src_lo=mov_lo, first=True,
                        last=True, each=None):
                pe.wait_ge(w_hi_ready, unit0 + 1 + RING * rounds)
                hi_passes(dst, unit0, src_hi, src_lo, ks, first, each)
                pe.wait_ge(w_lo_ready, unit0 + 1 + RING * rounds)
                lo_passes(dst, unit0, src_hi, ks, last).then_inc(passes, 1)

            def filled(fill):
                return lambda n: pe.wait_ge(lo_ready, 8 * fill + n + 1)

            def sum_squares(z):
                step(pe, added, z, "t7")
                pe.matmul(bank[7][:], ones, sqsum[:], start=True, stop=True).then_inc(norm_sum, 1)

            def head_sum(n):
                pe.wait_ge(hd_sq, n + 1)
                step(pe, hd_norm, n - 1, "log")
                pe.matmul(bank[2][:], c_(C0_HALF), hsq[:, n % 2, :], start=True,
                          stop=True).then_inc(hd_sum, 1)

            def head_rot(n):
                pe.wait_ge(hd_gain, n + 1)
                step(pe, hd_rope, n - 1, "sin")
                pe.matmul(bank[3][:], c_(C0_ROT), qk[:, n, :], start=True, stop=True).then_inc(hd_rot, 1)

            def turn_v():
                pe.wait_ge(taken, E_IN0 + 6)
                pe.wait_ge(rstd_ready, 1)
                for b in range(NB):
                    mm = pe.transpose(bank[7][:, b * P:(b + 1) * P], vT[:, b * P:(b + 1) * P], ident[0])
                mm.then_inc(v_turned, 1)

            def scores(n):
                b, g = divmod(n, 2)
                step(pe, hd_rope, 4, "sum")
                step(pe, sm_max, n - 1, "join")
                step(pe, sm_exp, n - 2, "e3")
                rows = slice(g * HEAD, (g + 1) * HEAD)
                for t in range(4):
                    q = qk[rows, t, b * P:(b + 1) * P]
                    if b:
                        pe.matmul(bank[4][:, t * P:(t + 1) * P], q, qk[rows, 4, (b - 1) * P:b * P],
                                  start=True, stop=True)
                    mm = pe.matmul(bank[5 + g][:, t * P:(t + 1) * P], q, qk[rows, 4, b * P:(b + 1) * P],
                                   start=True, stop=True)
                mm.then_inc(scored, 1)

            def turn_probs(n):
                pe.wait_ge(sm_div, n + 1)
                pe.wait_ge(v_tok, 1)
                step(pe, sm_mask, n - 1, "prev")
                for t in range(4):
                    mm = pe.transpose(bank[7][:, t * P:(t + 1) * P], prob[:, n % 2, t, :], ident[0])
                mm.then_inc(turned, 1)

            def pv(n):
                b, g = divmod(n, 2)
                step(pe, sm_mask, n, "prev")
                many(pe, y_copied, b - 1)
                rows = slice(g * HEAD, (g + 1) * HEAD)
                y = bank[2 + b % 2]
                for t in range(4):
                    if b:
                        pe.matmul(y[rows, t * P:(t + 1) * P], vtok[:, b - 1, rows],
                                  probT[:, n % 2, 0, t, :], start=True, stop=False)
                    mm = pe.matmul(y[rows, t * P:(t + 1) * P], vtok[:, b, rows],
                                   probT[:, n % 2, 1, t, :], start=b == 0, stop=True)
                mm.then_inc(pv_done, 1)

            pe.wait_ge(kept_loaded, 16)
            for n in range(IN0_UNITS):
                many(pe, taken, n - 1)
                project(bank[n % 2][:], U_IN0 + n, 0, each=filled(0) if n == 0 else None)
                if n == 0:
                    sum_squares(0)
                if n == 2:
                    pe.wait_ge(cst_loaded, 16)
                if 2 <= n <= 6:
                    head_sum(n - 2)
                if 3 <= n <= 7:
                    head_rot(n - 3)
                if n == 7:
                    turn_v()
                if 8 <= n < 16:
                    scores(n - 8)
                if 10 <= n:
                    turn_probs(n - 10)
                if 11 <= n:
                    pv(n - 11)
            pv(7)

            def out_project(u0, e0, fill, order):
                for m in range(KT):
                    pe.wait_ge(taken, e0 + max(m - 1, 0))
                    project(bank[m % 2][:], u0 + m, 0, ks=order, each=filled(fill) if m == 0 else None)

            out_project(U_OUT0, E_OUT0, 1, MIX_ORDER)

            def ffn(u_gu, e_gu, u_down, e_down, z, fill, blk0):
                def gate_up(unit0, rounds, e_at, first=False):
                    for t in range(4):
                        if not first:
                            pe.wait_ge(taken, e_at + t + 1)
                        project(bank[t][:], unit0 + t, rounds,
                                each=filled(fill) if first and t == 0 else None)
                        if first and t == 0:
                            sum_squares(z)

                pe.wait_ge(taken, e_gu)
                gate_up(u_gu, 0, None, first=True)
                with pe.Fori(0, 10) as i:
                    gate_up(u_gu + 4, i, e_gu + 4 * i)
                pe.wait_ge(taken, e_down)
                pe.wait_ge(act_lo_ready, 2 * (blk0 + 11))
                with pe.Fori(0, 4) as i:
                    for m in range(2):
                        for half in range(2):
                            if half == 0:
                                pe.wait_ge(taken, e_down + m - 1 + 2 * i)
                            part = slice(half * FH, (half + 1) * FH)
                            project(bank[m][:], u_down + 2 * m + half, i, range(FH),
                                    act_hi[:, part, :], act_lo[:, part, :],
                                    first=half == 0, last=half == 1)

            ffn(U_GU0, E_GU0, U_DOWN0, E_DOWN0, 1, 2, 0)

            pe.wait_ge(taken, E_IN1)
            pe.wait_ge(prm_loaded, 16)
            for k in range(KT):
                pe.wait_ge(gt_x, k + 1)
                pe.matmul(bank[6][0:16, :], prm[:, R_BA + 16 * k:R_BA + 16 * (k + 1)],
                          (gam, gamL)[k % 2][:].rearrange("p c n -> p (c n)"), start=k == 0,
                          stop=k == KT - 1).then_inc(gt_x_used, 1)
            sum_squares(2)
            pe.wait_ge(cst_loaded, 32)
            step(pe, gt_vec, 0, "scaled")
            for c in range(NB):
                mm = pe.transpose(bank[5][:, 16 * c:16 * (c + 1)], ba[:, c * P:(c + 1) * P],
                                  cst1[0:16, C_ID:C_ID + 16])
            mm.then_inc(gt_pe.sem, 1)

            def gate_cumsum():
                step(pe, gt_vec, 0, "g")
                pe.matmul(bank[6][:, 0:32], upper[1], flat(sm[:, 6]), start=True,
                          stop=True).then_inc(gt_pe.sem, 1)

            def project_quarter(n, j):
                tile, part = divmod(j, 4)
                dst = bank[tile % 2][:]
                if part == 0:
                    if not isinstance(n, int) or n or tile > 1:
                        pe.wait_ge(taken, E_IN1 - 1 + tile + 4 * n)
                    pe.wait_ge(w_hi_ready, U_IN1 + tile + 1 + 4 * n)
                if part < 3:
                    ks = (range(0, 3), range(3, 6), range(6, 8))[part]
                    hi_passes(dst, U_IN1 + tile, mov_hi, mov_lo, ks, first=part == 0,
                              each=(lambda _, k0=ks[0]: pe.wait_ge(lo_ready, 8 * 3 + k0 + len(ks)))
                              if isinstance(n, int) and n == 0 and tile == 0 else None)
                else:
                    pe.wait_ge(w_lo_ready, U_IN1 + tile + 1 + 4 * n)
                    lo_passes(dst, U_IN1 + tile, mov_hi, range(KT), last=True).then_inc(passes, 1)

            def prep_sums(n):
                step(pe, pr_act, n, "sqk")
                step(pe, pr_vec, n - 1, "kdec")
                pe.matmul(bank[5][:], ones, nsq[:, 0, :], start=True, stop=True).then_inc(pr_pe.sem, 1)
                step(pe, pr_vec, n - 1, "bv")
                pe.matmul(bank[4][:], ones, nsq[:, 1, :], start=True, stop=True).then_inc(pr_pe.sem, 1)

            def prep_rows(n, par):
                step(pe, pr_act, n, "lnk")
                for c in range(NB):
                    mm = pe.matmul(bank[4][:, c * P:(c + 1) * P],
                                   hp[:, par, H_G + c:H_G + c + 1].to_broadcast([P, P]), upper[1],
                                   start=True, stop=True)
                mm.then_inc(pr_pe.sem, 1)

            def prep_gram(n, par):
                step(pe, pr_vec, n, "kn")
                for c in range(NB):
                    kc = qkv[:, par, 1, c * P:(c + 1) * P]
                    mm = pe.matmul(bank[5][:, c * P:(c + 1) * P], kc, kc, start=True, stop=True)
                mm.then_inc(pr_pe.sem, 1)

            def prep_turn_a(n):
                step(pe, pr_vec, n, "A3")
                for c in range(NB):
                    mm = pe.transpose(bank[5][:, c * P:(c + 1) * P], nA[:, c, :], ident[1])
                mm.then_inc(pr_pe.sem, 1)

            def prep_qk(n, par):
                step(pe, pr_act, n, "eR")
                step(pe, pr_vec, n, "qn")
                for c in range(NB):
                    mm = pe.matmul(bank[4][:, c * P:(c + 1) * P], qkv[:, par, 1, c * P:(c + 1) * P],
                                   qkv[:, par, 0, c * P:(c + 1) * P], start=True, stop=True)
                mm.then_inc(pr_pe.sem, 1)

            def prep_turn_kv(n, par, part):
                step(pe, pr_vec, n, "WT" if part == 1 else "att")
                dst = bank[5] if part == 1 else bank[4]
                for c in range(NB):
                    mm = pe.transpose(dst[:, c * P:(c + 1) * P], qkv[:, par, part, c * P:(c + 1) * P],
                                      ident[1])
                mm.then_inc(pr_pe.sem, 1)

            def inv_y(n, par, lvl):
                if lvl == 1:
                    step(pe, pr_vec, n, "R")
                    step(pe, iv_vec, n - 1, "M6")
                else:
                    step(pe, iv_vec, n, f"R{lvl - 1}")
                for q in range(2):
                    mm = pe.matmul(bank[2][:, q * P:(q + 1) * P], W[:, par, q, :], R[:, par, q, :],
                                   start=True, stop=True)
                mm.then_inc(iv_pe.sem, 1)

            def inv_z(n, par, lvl):
                step(pe, iv_vec, n, f"Y{lvl}")
                if lvl == 1:
                    step(pe, pr_pool, n, "V")
                    step(pe, iv_vec, n - 1, "T6")
                else:
                    step(pe, iv_vec, n, f"V{lvl - 1}")
                for q in range(2):
                    mm = pe.matmul(bank[2][:, (q + 2) * P:(q + 3) * P], V[:, par, q, :], Y[:, q, :],
                                   start=True, stop=True)
                mm.then_inc(iv_pe.sem, 1)
                for q in range(2):
                    mm = pe.matmul(bank[3][:, q * P:(q + 1) * P], Y[:, q, :], V[:, par, q, :],
                                   start=True, stop=True)
                mm.then_inc(iv_pe.sem, 1)

            def scan_k(n, par, c):
                step(pe, sc_vec, n, f"S{c - 1}")
                pe.matmul(bank[6][:, 0:P], kd[:, par, c * P:(c + 1) * P], S[:], start=True,
                          stop=True).then_inc(sc_pe.sem, 1)

            def scan_v(n, par, c):
                if c == 0:
                    step(pe, iv_vec, n, "XA")
                    step(pe, sc_act, n - 1, "log")
                    rhs = bv[:, par, 0, :]
                else:
                    step(pe, sc_vec, n, f"r{c}")
                    rhs = R1[:]
                pe.matmul(bank[6][:, P:2 * P], XT[:, par, c, :], rhs, start=True,
                          stop=True).then_inc(sc_pe.sem, 1)

            def scan_o(n, par, c):
                if c == 0:
                    step(pe, sc_vec, n - 1, "gain")
                    step(pe, pr_pool, n, "qd")
                step(pe, sc_vec, n, f"vn{c}")
                o = bank[7][:, c * P:(c + 1) * P]
                if c:
                    pe.matmul(o, S[:], qd[:, par, c * P:(c + 1) * P], start=True, stop=False)
                mm = pe.matmul(o, vn[:], attT[:, par, c, :], start=c == 0, stop=True)
                if c < NB - 1:
                    mm = pe.matmul(bank[6][:, 2 * P:3 * P], kdec[:, par, c, :], vn[:], start=True,
                                   stop=True)
                mm.then_inc(sc_pe.sem, 1)

            def scan_sum(n):
                step(pe, sc_act, n, "sq")
                pe.matmul(bank[6][:], ones, osq, start=True, stop=True).then_inc(sc_pe.sem, 1)

            def period(n, par, rounds, proj, prep, inv, scan):
                other = 1 - par
                for j in range(16):
                    if proj:
                        project_quarter(n, j)
                        if isinstance(n, int) and n == 0 and j == 5:
                            gate_cumsum()
                    if prep and j == 0:
                        prep_sums(n - 1)
                    if inv:
                        if j in INV_Y:
                            inv_y(n - 2, par, INV_Y.index(j) + 1)
                        if j in INV_Z:
                            inv_z(n - 2, par, INV_Z.index(j) + 1)
                    if scan:
                        if j in SCAN_K:
                            scan_k(n - 3, other, SCAN_K.index(j) + 1)
                        if j in SCAN_V:
                            scan_v(n - 3, other, SCAN_V.index(j))
                        if j in SCAN_O:
                            scan_o(n - 3, other, SCAN_O.index(j))
                        if j == 13:
                            scan_sum(n - 3)
                    if prep:
                        if j == 3:
                            prep_rows(n - 1, other)
                        if j == 6:
                            prep_gram(n - 1, other)
                        if j == 9:
                            prep_turn_a(n - 1)
                        if j == 12:
                            prep_qk(n - 1, other)
                        if j == 13:
                            prep_turn_kv(n - 1, other, 1)
                        if j == 14:
                            prep_turn_kv(n - 1, other, 2)

            all_periods(pe, period)

            out_project(U_OUT1, E_OUT1, 4, range(KT))
            ffn(U_GU1, E_GU1, U_DOWN1, E_DOWN1, 3, 5, 11)

        @block.vector
        def _(dve):
            def gain_col(z, m):
                return prm[:, bass.ds(R_GAIN + 8 * z + m, 1)]

            def lo_of_x(count, lo, hi, xm, gain):
                dve.wait_ge(hi_ready, count)
                dve.scalar_tensor_tensor(out=lo, in0=xm, scalar=gain, in1=hi.bitcast(F32),
                                         op0=ALU.mult, op1=ALU.subtract).then_inc(lo_ready, 1)

            def fill_from_x(fill, z):
                for m in range(KT):
                    lo_of_x(8 * fill + m + 1, mov_lo[:, m, :], mov_hi[:, m, :], x[:, m, :],
                            gain_col(z, m))

            def fill_from(fill, n, src, k):
                dve.wait_ge(hi_ready, 8 * fill + n + 1)
                dve.tensor_tensor(mov_lo[:, k, :], src[:, k, :], mov_hi[:, k, :].bitcast(F32),
                                  ALU.subtract).then_inc(lo_ready, 1)

            dve.wait_ge(prm_loaded, 16)
            fill_from_x(0, 0)
            dve.tensor_scalar(nsink[:], prm[:, R_SINK:R_SINK + 8], -1.0, None,
                              ALU.mult).then_inc(nsink_ready, 1)
            for j in range(2):
                dve.memset(cx[:, j, 0:2], 0.0).then_inc(pad0, 1)

            dve.wait_ge(cst_loaded, 16)
            dve.wait_ge(rstd_ready, 1)
            dve.tensor_tensor(rstd2[:], rstd[:], rstd[:], ALU.mult).then_inc(rstd2_ready, 1)
            dve.wait_ge(rstd2_ready, 1)

            def head_gain(n):
                step(dve, hd_norm, n, "rsqrt")
                g = prm[:, R_QG:R_QG + 1] if n < 4 else prm[:, R_KG:R_KG + 1]
                dve.scalar_tensor_tensor(out=qk[:, n, :], in0=qk[:, n, :], scalar=g,
                                         in1=hrs[:, n % 2, :], op0=ALU.mult,
                                         op1=ALU.mult).then_inc(hd_gain, 1)

            def head_rope(n):
                dve.wait_ge(hd_rot, n + 1)
                step(dve, hd_rope, n - 1, "sum")
                dve.tensor_tensor(rope_s[:], bank[3][:], c_(C0_SIN, 0, T),
                                  ALU.mult).then_inc(hd_rope.sem, 1)
                dve.wait_ge(hd_cos, n + 1)
                step(dve, hd_rope, n, "sin")
                dve.tensor_tensor(qk[:, n, :], rope_c[:, n % 2, :], rope_s[:],
                                  ALU.add).then_inc(hd_rope.sem, 1)

            def take_conv(n):
                grp, r = divmod(n - 6, 6)
                kind, t = divmod(r, 2)
                c = 2 * grp + t
                dve.wait_ge(passes, n + 1)
                src = bank[n % 2][:]
                if kind == 0:
                    dve.tensor_tensor(gate_c[:, t, :], src, rstd2[:], ALU.mult).then_inc(taken, 1)
                elif kind == 1:
                    step(dve, cc_vec, c - 2, "tap2")
                    dve.wait_ge(pad0, 2)
                    dve.wait_ge(taken, n - 1)
                    dve.tensor_tensor(cx[:, t, 2:T + 2], src, gate_c[:, t, :],
                                      ALU.mult).then_inc(taken, 1)
                else:
                    dve.wait_ge(cc_scale, c + 1)
                    dve.tensor_tensor(mix[:, 4 + c, :], src, conv0[:, t, :],
                                      ALU.mult).then_inc(taken, 1)

            def conv_taps(c):
                dve.wait_ge(cc_tap, c + 1)
                t = c % 2
                for j in (1, 2):
                    if j == 2:
                        step(dve, cc_vec, c, "tap1")
                    dve.scalar_tensor_tensor(out=conv0[:, t, :], in0=cx[:, t, j:j + T],
                                             scalar=prm[:, R_CONV0 + 3 * c + j:R_CONV0 + 3 * c + j + 1],
                                             in1=conv0[:, t, :], op0=ALU.mult,
                                             op1=ALU.add).then_inc(cc_vec.sem, 1)

            def softmax_max(n):
                b, g = divmod(n, 2)
                r = n % 2
                cur = chunks(bank[5 + g][:])
                dve.wait_ge(scored, n + 1)
                mask = over_chunks(c_(C0_SUP).bitcast(U32))
                data = chunks(bank[4][:]) if b else c_(C0_NEG, 0, 1).unsqueeze(2).to_broadcast([P, 4, P])
                dve.copy_predicated(cur, mask, data).then_inc(sm_max.sem, 1)
                step(dve, sm_max, n, "join")
                dve.tensor_reduce(mx[:, r, :], cur, AX.X, ALU.max).then_inc(sm_max.sem, 1)
                step(dve, sm_max, n, "max")
                dve.wait_ge(nsink_ready, 1)
                dve.scalar_tensor_tensor(out=nmx[:, r, :], in0=mx[:, r, :], scalar=-(HEAD ** -0.5),
                                         in1=nsink[:, 4 * g:4 * g + 4], op0=ALU.mult,
                                         op1=ALU.min).then_inc(sm_max.sem, 1)
                step(dve, sm_max, n, "neg")
                dve.tensor_tensor(sgap[:, r, :], prm[:, R_SINK + 4 * g:R_SINK + 4 * g + 4], nmx[:, r, :],
                                  ALU.add).then_inc(sm_max.sem, 1)

            def softmax_den(n):
                r = n % 2
                step(dve, sm_exp, n, "sink")
                dve.tensor_tensor(den2[:, r, :], den[:, r, :], esink[:, r, :],
                                  ALU.add).then_inc(sm_den.sem, 1)
                step(dve, sm_den, n, "sum")
                dve.reciprocal(rden[:, r, :], den2[:, r, :]).then_inc(sm_den.sem, 1)

            def softmax_mask(n):
                r = n % 2
                dve.wait_ge(turned, n + 1)
                many(dve, pv_done, n - 1)
                pt = chunks(bank[7][:])
                dve.tensor_tensor(probT[:, r, 1], pt, over_chunks(upper[0]), ALU.mult).then_inc(sm_mask.sem, 1)
                dve.tensor_tensor(probT[:, r, 0], pt, over_chunks(lower[0]), ALU.mult).then_inc(sm_mask.sem, 1)

            for n in range(18):
                if 9 <= n <= 16:
                    softmax_den(n - 9)
                if n < 6:
                    dve.wait_ge(passes, n + 1)
                    dst = qk[:, n, :] if n < 5 else vT[:]
                    dve.tensor_tensor(dst, bank[n % 2][:], rstd[:], ALU.mult).then_inc(taken, 1)
                else:
                    take_conv(n)
                if 2 <= n <= 6:
                    head_gain(n - 2)
                if 3 <= n <= 7:
                    head_rope(n - 3)
                if 8 <= n < 16:
                    softmax_max(n - 8)
                if n in (8, 9, 14, 15):
                    conv_taps(n - 8 if n < 10 else n - 12)
                if 10 <= n:
                    softmax_mask(n - 10)
            for n, k in enumerate(MIX_ORDER):
                fill_from(1, n, mix, k)

            def residual(xm, src, npass):
                dve.wait_ge(passes, npass)
                dve.tensor_tensor(xm, src, xm, ALU.add).then_inc(taken, 1)

            def out_project(u0, z, fill):
                for m in range(KT):
                    residual(x[:, m, :], bank[m % 2][:], u0 + m + 1)
                fill_from_x(fill, z)

            def ffn(u_gu, e_gu, u_down, e_down, z, blk0, nz, fill):
                def block_(u0, blk, at, e_at):
                    for t in range(2):
                        dve.wait_ge(passes, u0 + t + 1)
                        many(dve, gated, 2 * blk + t - 1)
                        dve.tensor_tensor(gs[:, t, :], bank[t][:], rstd[:], ALU.mult).then_inc(taken, 1)
                    for t in range(2):
                        dve.wait_ge(passes, u0 + 3 + t)
                        many(dve, act_lo_ready, 2 * blk + t - 1)
                        dve.tensor_tensor(us[:, t, :], bank[2 + t][:], rstd[:], ALU.mult).then_inc(taken, 1)
                        dve.wait_ge(silu_g, 2 * blk + t + 1)
                        dve.wait_ge(taken, e_at + 3 + t)
                        dve.tensor_tensor(us[:, t, :], us[:, t, :], gs[:, t, :], ALU.mult).then_inc(gated, 1)
                    for t in range(2):
                        dve.wait_ge(act_hi_ready, 2 * blk + t + 1)
                        dve.wait_ge(gated, 2 * blk + t + 1)
                        dve.tensor_tensor(at(act_lo, t), us[:, t, :], at(act_hi, t).bitcast(F32),
                                          ALU.subtract).then_inc(act_lo_ready, 1)

                dve.wait_ge(rstd_ready, z + 1)
                block_(u_gu, blk0, lambda a, t: a[:, t, :], e_gu)
                with dve.Fori(0, 10) as i:
                    block_(u_gu + 4 + 4 * i, blk0 + 1 + i,
                           lambda a, t: a[:, bass.ds(2 * i + (2 + t), 1), :].rearrange("p a n -> p (a n)"),
                           e_gu + 4 + 4 * i)
                with dve.Fori(0, 4) as i:
                    for m in range(2):
                        at = bass.ds(2 * i + m, 1)
                        xm = x[:, at, :].rearrange("p a n -> p (a n)")
                        residual(xm, bank[m][:], u_down + 2 * m + 2 + 4 * i)
                        if nz is not None:
                            lo_of_x(8 * fill + m + 1 + 2 * i,
                                    mov_lo[:, at, :].rearrange("p a n -> p (a n)"),
                                    mov_hi[:, at, :].rearrange("p a n -> p (a n)"), xm,
                                    gain_col(nz, m + 2 * i))

            out_project(U_OUT0, 1, 2)
            ffn(U_GU0, E_GU0, U_DOWN0, E_DOWN0, 1, 0, 2, 3)

            def gate(ins):
                ins.then_inc(gt_vec.sem, 1)

            def after_gate(name):
                step(dve, gt_vec, 0, name)

            dve.wait_ge(passes, U_IN1)
            for k in range(KT):
                many(dve, gt_x_used, k - 1)
                dve.wait_ge(taken, E_IN1)
                dve.tensor_scalar((gam, gamL)[k % 2][:].rearrange("p c n -> p (c n)"), x[:, k, :],
                                  gain_col(2, k), None, ALU.mult).then_inc(gt_x, 1)
            for j in range(3):
                dve.memset(u[:, j, 0:3], 0.0).then_inc(zeroed, 1)
            dve.wait_ge(gt_x_used, KT)
            dve.wait_ge(rstd_ready, 3)
            gate(dve.tensor_tensor(ba, bank[6][0:16, :], rstd[0:16, :], ALU.mult))
            step(dve, gt_pe, 0, "turned")
            gate(dve.tensor_copy(flat(bt[:]), bank[5][:, 0:64]))
            gate(dve.tensor_copy(HP[:, :, 0:12],
                                 prm[:, R_HEAD:R_HEAD + 96].rearrange("p (h n) -> p h n", n=12)))
            step(dve, gt_act, 0, "ebeta")
            gate(dve.tensor_scalar(sm[:, 1], sm[:, 0], 1.0, None, ALU.add))
            after_gate("plus1")
            gate(dve.reciprocal(sm[:, 2], sm[:, 1]))
            after_gate("beta")
            by_head = sm[:, 2].rearrange("p c h -> p h c")
            gate(dve.tensor_copy(HP[:, :, H_BETA:H_BETA + NB], by_head))
            gate(dve.tensor_scalar(HP[:, :, H_NBETA:H_NBETA + NB], by_head, -1.0, None, ALU.mult))
            gate(dve.tensor_tensor(sm[:, 3], bt[:, :, 8:16], over_chunks(prm[:, R_DT:R_DT + 8]), ALU.add))
            after_gate("z")
            gate(dve.scalar_tensor_tensor(out=sm[:, 4], in0=sm[:, 3], scalar=-1.0, in1=sm[:, 3],
                                          op0=ALU.mult, op1=ALU.min))
            gate(dve.tensor_scalar(sm[:, 7], sm[:, 3], 0.0, None, ALU.max))
            step(dve, gt_act, 0, "log")
            after_gate("relu")
            gate(dve.tensor_tensor(sm[:, 1], sm[:, 7], sm[:, 5], ALU.add))
            after_gate("softplus")
            gate(dve.scalar_tensor_tensor(out=sm[:, 6], in0=sm[:, 1], scalar=-1.0,
                                          in1=over_chunks(esum[:]), op0=ALU.mult, op1=ALU.mult))
            after_gate("g")
            gate(dve.tensor_copy(HP[:, :, H_G:H_G + NB], sm[:, 6].rearrange("p c h -> p h c")))
            step(dve, gt_pe, 0, "cum")
            gate(dve.tensor_copy(HP[:, :, H_GC:H_GC + NB],
                                 bank[6][:, 0:32].rearrange("p (c h) -> p h c", h=8)))
            after_gate("gc_h")

            def take(n, tile):
                dve.wait_ge(passes, U_IN1 + tile + 1 + 4 * n)
                src = bank[tile % 2][:]
                if tile < 3:
                    step(dve, taps, n - 1, ("q3", "k3", "v3")[tile])
                    if isinstance(n, int) and n == 0:
                        dve.wait_ge(zeroed, 3)
                    dst = u[:, tile, 3:T + 3]
                else:
                    dst = dno[:, bass.ds(n, 1), :].rearrange("p a n -> p (a n)")
                dve.tensor_tensor(dst, src, rstd[:], ALU.mult).then_inc(taken, 1)

            def conv_tap(n, par, part, j):
                if j == 1:
                    step(dve, tap0, n, "qkv"[part])
                else:
                    step(dve, taps, n, "qkv"[part] + str(j - 1))
                dve.scalar_tensor_tensor(out=qkv[:, par, part, :], in0=u[:, part, j:j + T],
                                         scalar=hp[:, par, H_TAP + 4 * part + j:H_TAP + 4 * part + j + 1],
                                         in1=qkv[:, par, part, :], op0=ALU.mult,
                                         op1=ALU.add).then_inc(taps.sem, 1)

            def prep(ins):
                ins.then_inc(pr_vec.sem, 1)

            def prep_norms(n, par):
                step(dve, pr_act, n, "rsk")
                prep(dve.tensor_tensor(qkv[:, par, 1, :], qkv[:, par, 1, :], nrs[:, 1, :], ALU.mult))
                prep(dve.scalar_tensor_tensor(out=qkv[:, par, 0, :], in0=qkv[:, par, 0, :],
                                              scalar=float(P) ** -0.5, in1=nrs[:, 0, :], op0=ALU.mult,
                                              op1=ALU.mult))

            def prep_gaps(n, par):
                step(dve, pr_pe, n, "rows")
                step(dve, pr_vec, n - 1, "kdec")
                step(dve, pr_pool, n - 1, "gamU")
                for c in range(NB):
                    prep(dve.tensor_scalar(gam[:, c, :], bank[4][:, c * P:(c + 1) * P],
                                           hp[:, par, H_GC + c:H_GC + c + 1], None, ALU.subtract))

            def prep_gap(n):
                step(dve, pr_vec, n, "d3")
                prep(dve.scalar_tensor_tensor(out=gam[:], in0=gam[:], scalar=-1.0, in1=gam[:],
                                              op0=ALU.mult, op1=ALU.min))

            def prep_a(n, par):
                step(dve, pr_pe, n, "gram")
                step(dve, pr_pool, n, "gamL")
                step(dve, pr_pe, n - 1, "turnA")
                for c in range(NB):
                    prep(dve.scalar_tensor_tensor(out=nA[:, c, :], in0=bank[5][:, c * P:(c + 1) * P],
                                                  scalar=hp[:, par, H_NBETA + c:H_NBETA + c + 1],
                                                  in1=gamL[:, c, :], op0=ALU.mult, op1=ALU.mult))

            def diag(lvl):
                return over_chunks(c_(C1_DIAG + P * (lvl - 1), 1), 2)

            def prep_att(n, par):
                step(dve, sc_pe, n - 2, "o3")
                step(dve, pr_pe, n, "qk")
                step(dve, pr_pool, n, "gamU")
                prep(dve.tensor_tensor(attT[:, par], chunks(bank[4][:]), gamU[:], ALU.mult))

            def prep_w(n, par):
                step(dve, pr_pe, n, "turnA")
                aT = bank[5][:].rearrange("p (q two n) -> p q two n", two=2, n=P)
                a = nA[:].rearrange("p (q two) n -> p q two n", two=2)
                prep(dve.tensor_tensor(W[:, par], aT[:, :, 0], a[:, :, 1], ALU.add))
                prep(dve.tensor_tensor(WT[:], aT[:, :, 1], a[:, :, 0], ALU.add))

            def prep_m(n, par):
                step(dve, pr_vec, n, "WT")
                prep(dve.tensor_tensor(M[:, par], WT[:], over_chunks(c_(C1_PAIR, 1), 2), ALU.mult))
                step(dve, pr_vec, n, "m")
                prep(dve.tensor_tensor(M[:, par], M[:, par], over_chunks(ident[1], 2), ALU.add))
                step(dve, pr_vec, n, "M")
                prep(dve.tensor_tensor(R[:, par], M[:, par], diag(1), ALU.mult))

            def prep_k(n, par):
                step(dve, pr_pe, n, "turnK")
                step(dve, pr_act, n, "gam")
                prep(dve.tensor_tensor(kdec[:, par], chunks(bank[5][:]),
                                       gam[:, :, P - 1:P].to_broadcast([P, NB, P]), ALU.mult))

            def prep_v(n, par):
                step(dve, pr_pe, n, "turnV")
                prep(dve.tensor_tensor(bv[:, par], chunks(bank[4][:]),
                                       along(hp[:, par, H_BETA:H_BETA + NB]), ALU.mult))
                prep(dve.tensor_copy(decb[:, par, :], chunks(eR[:])[:, :, P - 1]))
                prep(dve.tensor_copy(betab[:, par, :], hp[:, par, H_NBETA:H_NBETA + NB]))

            def inv(ins):
                ins.then_inc(iv_vec.sem, 1)

            def inv_y(n, par, lvl):
                step(dve, iv_pe, n, f"Y{lvl}")
                off = over_chunks(c_(C1_OFF + P * (lvl - 1), 1), 2)
                inv(dve.tensor_tensor(Y[:], pairs(bank[2][:, 0:2 * P]), off, ALU.mult))

            def inv_x(n, par, lvl):
                xt = XT[:, par].rearrange("p (q two) n -> p q two n", two=2)
                step(dve, iv_pe, n, f"Z{lvl}")
                inv(dve.tensor_tensor(M[:, par], pairs(bank[2][:, 2 * P:]), M[:, par], ALU.add))
                step(dve, iv_vec, n, f"M{lvl}")
                if lvl < 6:
                    inv(dve.tensor_tensor(R[:, par], M[:, par], diag(lvl + 1), ALU.mult))
                else:
                    step(dve, sc_pe, n - 2, "o3")
                    inv(dve.tensor_tensor(xt[:, :, 1], M[:, par], over_chunks(upper[1], 2), ALU.mult))
                step(dve, iv_pe, n, f"T{lvl}")
                if lvl == 1:
                    step(dve, pr_pool, n, "V")
                inv(dve.tensor_tensor(MT[:, par], pairs(bank[3][:, 0:2 * P]), MT[:, par], ALU.add))
                step(dve, iv_vec, n, f"T{lvl}")
                if lvl < 6:
                    inv(dve.tensor_tensor(V[:, par], MT[:, par], diag(lvl + 1), ALU.mult))
                else:
                    inv(dve.tensor_tensor(xt[:, :, 0], MT[:, par], over_chunks(upper[1], 2), ALU.mult))

            def scan(ins):
                ins.then_inc(sc_vec.sem, 1)

            def scan_r(n, par, c):
                step(dve, sc_pe, n, f"k{c}")
                step(dve, sc_pe, n, f"v{c - 1}")
                step(dve, pr_vec, n, "beta")
                scan(dve.scalar_tensor_tensor(out=R1[:], in0=bank[6][:, 0:P],
                                              scalar=betab[:, par, c:c + 1], in1=bv[:, par, c, :],
                                              op0=ALU.mult, op1=ALU.add))

            def scan_vn(n, par, c):
                step(dve, sc_pe, n, f"v{c}")
                step(dve, sc_pe, n - 1 if c == 0 else n, "o3" if c == 0 else f"o{c - 1}")
                scan(dve.tensor_copy(vn[:], bank[6][:, P:2 * P]))

            def scan_s(n, par, c):
                step(dve, sc_pe, n, f"o{c}")
                if c == 0:
                    scan(dve.tensor_copy(S[:], bank[6][:, 2 * P:3 * P]))
                else:
                    scan(dve.scalar_tensor_tensor(out=S[:], in0=S[:], scalar=decb[:, par, c:c + 1],
                                                  in1=bank[6][:, 2 * P:3 * P], op0=ALU.mult,
                                                  op1=ALU.add))

            def scan_gain(n):
                step(dve, sc_act, n, "sq")
                step(dve, silu, n + 1, "z")
                step(dve, sc_vec, n - 1, "out")
                z = dno[:, bass.ds(n, 1), :].rearrange("p a n -> p (a n)")
                scan(dve.scalar_tensor_tensor(out=og, in0=bank[7][:], scalar=prm[:, R_OG:R_OG + 1],
                                              in1=z, op0=ALU.mult, op1=ALU.mult))

            def scan_out(n):
                step(dve, sc_act, n, "rs")
                step(dve, sc_vec, n, "gain")
                z = dno[:, bass.ds(n, 1), :].rearrange("p a n -> p (a n)")
                scan(dve.tensor_tensor(z, og, ors[:], ALU.mult))

            def period(n, par, rounds, proj_, prep_, inv, scan_):
                other = 1 - par
                if proj_:
                    step(dve, taps, n - 2, "v3")
                    step(dve, pr_vec, n - 2, "beta")
                    dve.tensor_copy(hp[:, par, :], HP[:, bass.ds(n, 1), :].rearrange("p a n -> p (a n)")
                                    ).then_inc(fetched, 1)
                for j in range(16):
                    if inv:
                        if j in INV_Y:
                            inv_y(n - 2, par, INV_Y.index(j) + 1)
                        if j in INV_Z:
                            inv_x(n - 2, par, INV_Z.index(j) + 1)
                    if scan_:
                        if j in SCAN_K:
                            scan_r(n - 3, other, SCAN_K.index(j) + 1)
                        if j in SCAN_V:
                            scan_vn(n - 3, other, SCAN_V.index(j))
                        if j in SCAN_O and j != SCAN_O[3]:
                            scan_s(n - 3, other, SCAN_O.index(j))
                        if j == 12:
                            scan_gain(n - 3)
                    if prep_:
                        if j == 3:
                            prep_norms(n - 1, other)
                        if j == 4:
                            prep_gaps(n - 1, other)
                        if j == 5:
                            prep_gap(n - 1)
                        if j == 7:
                            prep_a(n - 1, other)
                        if j == 10:
                            prep_w(n - 1, other)
                        if j == 11:
                            prep_m(n - 1, other)
                        if j == 13:
                            prep_att(n - 1, other)
                        if j == 14:
                            prep_k(n - 1, other)
                        if j == 15:
                            prep_v(n - 1, other)
                    if proj_ and j % 4 == 3:
                        take(n, j // 4)
                    if proj_ and j in TAPS:
                        conv_tap(n, par, *TAPS[j])
                if scan_:
                    scan_out(n - 3)
                for k in {8: range(6), 9: (6,), 10: (7,)}.get(n if isinstance(n, int) else 0, ()):
                    fill_from(4, k, dno, k)

            all_periods(dve, period)
            out_project(U_OUT1, 3, 5)
            ffn(U_GU1, E_GU1, U_DOWN1, E_DOWN1, 3, 11, None, None)

        @block.scalar
        def _(act):
            def exp_table():
                act.preload_act_table_set("natural_log_exp_and_others")

            def silu_table():
                act.preload_act_table_set("silu_and_others")

            act.dma_start(prm[:], params).then_inc(prm_loaded, 16)
            for j in range(4):
                act.dma_start(flat(x[:, 2 * j:2 * j + 2, :]), xT[:, 2 * T * j:2 * T * (j + 1)]
                              ).then_inc(x_loaded[j], 16)
            act.dma_start(kpt[:], kept).then_inc(kept_loaded, 16)
            act.dma_start(cst0[:], consts0).then_inc(cst_loaded, 16)
            exp_table()

            def split(unit0, rounds=0):
                act.wait_ge(unit_loaded[unit0 % RING], 16 * (unit0 // RING + 1) + 16 * rounds)
                if not (isinstance(rounds, int) and unit0 + RING * rounds < 2):
                    act.wait_ge(passes, unit0 - 1 + RING * rounds)
                n = unit_tiles(unit0) * UW
                act.activation(w_hi[:, unit0 % 2, 0:n], raw[:, unit0 % RING, 0:n],
                               ACT.Copy).then_inc(w_hi_ready, 1)

            def round_x(hi, xm, gain):
                act.activation(hi, xm, ACT.Copy, scale=gain).then_inc(hi_ready, 1)

            def gain_col(z, m):
                return prm[:, bass.ds(R_GAIN + 8 * z + m, 1)]

            def fill_from(src, k):
                act.activation(mov_hi[:, k, :], src[:, k, :], ACT.Copy).then_inc(hi_ready, 1)

            def sq_free(z, m_abs):
                many(act, added.sem, 9 * z + m_abs)

            def square_x(m, xm):
                act.activation(sq[:, m % 2, :], xm, ACT.Square).then_inc(squared, 1)

            def rstd_of(z):
                act.wait_ge(norm_sum, z + 1)
                act.activation(rstd[:], bank[7][:], ACT.Ln, bias=eps_col,
                               scale=1.0 / D).then_inc(rstd_log, 1)
                act.wait_ge(rstd_log, z + 1)
                act.activation(rstd[:], rstd[:], ACT.Exp, scale=-0.5).then_inc(rstd_ready, 1)

            act.wait_ge(prm_loaded, 16)
            for m in range(KT):
                act.wait_ge(x_loaded[m // 2], 16)
                round_x(mov_hi[:, m, :], x[:, m, :], gain_col(0, m))
                if m == 0:
                    split(0)
            for m in range(KT):
                sq_free(0, m)
                square_x(m, x[:, m, :])
            split(1)
            act.wait_ge(kept_loaded, 16)
            rstd_of(0)

            def head_square(n):
                act.wait_ge(taken, n + 1)
                many(act, hd_sum, n - 1)
                act.activation(hsq[:, n % 2, :], qk[:, n, :], ACT.Square).then_inc(hd_sq, 1)

            def head_norm(n):
                act.wait_ge(hd_sum, n + 1)
                many(act, hd_gain, n - 1)
                act.activation(hrs[:, n % 2, :], bank[2][:], ACT.Ln, bias=eps_col,
                               scale=1.0 / HEAD).then_inc(hd_norm.sem, 1)
                step(act, hd_norm, n, "log")
                act.activation(hrs[:, n % 2, :], hrs[:, n % 2, :], ACT.Exp, scale=-0.5).then_inc(hd_norm.sem, 1)

            def first_tap(c):
                n = 8 + c if c < 2 else 12 + c
                act.wait_ge(taken, n + 1)
                many(act, taken, 10 + c - 2 + 1 if c > 1 else 0)
                act.activation(conv0[:, c % 2, :], cx[:, c % 2, 0:T], ACT.Copy,
                               scale=prm[:, R_CONV0 + 3 * c:R_CONV0 + 3 * c + 1]).then_inc(cc_tap, 1)

            def softmax_exp(n):
                g = n % 2
                r = n % 2
                step(act, sm_max, n, "neg")
                many(act, turned, n - 1)
                step(act, sm_den, n - 2, "sum")
                for t in range(4):
                    act.activation(prob[:, r, t, :], bank[5 + g][:, t * P:(t + 1) * P], ACT.Exp,
                                   bias=nmx[:, r, t:t + 1], scale=HEAD ** -0.5,
                                   accum_out=den[:, r, t:t + 1]).then_inc(sm_exp.sem, 1)
                step(act, sm_max, n, "gap")
                act.activation(esink[:, r, :], sgap[:, r, :], ACT.Exp).then_inc(sm_exp.sem, 1)

            for n in range(18):
                split(n + 2)
                if n < 5:
                    head_square(n)
                if 2 <= n <= 6:
                    head_norm(n - 2)
                if n in (8, 9, 14, 15):
                    first_tap(n - 8 if n < 10 else n - 12)
                if n == 7:
                    act.wait_ge(v_turned, 1)
                    act.activation(flat(vtok[:]), bank[7][:], ACT.Copy).then_inc(v_tok, 1)
                if 8 <= n < 16:
                    softmax_exp(n - 8)
                if n >= 12 and (n - 11) % 2 == 1:
                    b = (n - 12) // 2
                    act.wait_ge(pv_done, 2 * b + 2)
                    act.activation(mix[:, 0:4, b * P:(b + 1) * P], chunks(bank[2 + b % 2][:]),
                                   ACT.Copy).then_inc(y_copied, 1)
            act.wait_ge(passes, U_OUT0)
            act.wait_ge(taken, E_OUT0)
            for k in MIX_ORDER[0:4]:
                fill_from(mix, k)
            act.wait_ge(pv_done, 8)
            act.activation(mix[:, 0:4, 3 * P:4 * P], chunks(bank[3][:]), ACT.Copy).then_inc(y_copied, 1)
            act.wait_ge(y_copied, 4)
            for k in MIX_ORDER[4:8]:
                fill_from(mix, k)

            def out_project(u0, e0, z):
                for m in range(KT):
                    split(u0 + m + 2)
                    act.wait_ge(taken, e0 + m + 1)
                    sq_free(z, m)
                    square_x(m, x[:, m, :])
                for m in range(KT):
                    round_x(mov_hi[:, m, :], x[:, m, :], gain_col(z, m))
                rstd_of(z)

            def ffn(u_gu, e_gu, u_down, e_down, blk0, nz):
                def block_(unit0, rounds, blk, at, e_at):
                    for t in range(2):
                        split(unit0 + t + 2, rounds)
                        act.wait_ge(taken, e_at + t + 1)
                        act.activation(gs[:, t, :], gs[:, t, :], ACT.Silu).then_inc(silu_g, 1)
                    for t in range(2):
                        split(unit0 + t + 4, rounds)
                        act.wait_ge(gated, 2 * blk + t + 1)
                        act.activation(at(t), us[:, t, :], ACT.Copy).then_inc(act_hi_ready, 1)

                def down_(unit0, rounds, at, e_at, m_at):
                    for m in range(2):
                        for half in range(2):
                            if unit0 + 2 * m + half + 2 < U_END:
                                split(unit0 + 2 * m + half + 2, rounds)
                        xm = x[:, at(m), :].rearrange("p a n -> p (a n)")
                        if nz is not None:
                            sq_free(nz, m_at + m)
                        act.wait_ge(taken, e_at + m + 1)
                        if nz is None:
                            act.dma_start(outT[at(m), :, :].rearrange("a p n -> p (a n)"),
                                          xm).then_inc(out_done, 16)
                        else:
                            round_x(mov_hi[:, at(m), :].rearrange("p a n -> p (a n)"), xm,
                                    gain_col(nz, m_at + m))
                            square_x(m, xm)

                silu_table()
                block_(u_gu, 0, blk0, lambda t: act_hi[:, t, :], e_gu)
                with act.Fori(0, 9) as i:
                    block_(u_gu + 4, i, blk0 + 1 + i,
                           lambda t: act_hi[:, bass.ds(2 * i + (2 + t), 1), :].rearrange("p a n -> p (a n)"),
                           e_gu + 4 + 4 * i)
                block_(u_gu + 40, 0, blk0 + 10, lambda t: act_hi[:, 20 + t, :], e_gu + 40)
                with act.Fori(0, 3) as i:
                    down_(u_down, i, lambda m: bass.ds(2 * i + m, 1), e_down + 2 * i, 2 * i)
                down_(u_down + 12, 0, lambda m: bass.ds(6 + m, 1), e_down + 6, 6)
                exp_table()
                if nz is not None:
                    rstd_of(nz)

            out_project(U_OUT0, E_OUT0, 1)
            ffn(U_GU0, E_GU0, U_DOWN0, E_DOWN0, 0, 2)
            act.wait_ge(passes, U_IN1)
            act.dma_start(cst1[:], consts1).then_inc(cst_loaded, 16)

            act.activation(esum[:], prm[:, R_ALOG:R_ALOG + 8], ACT.Exp).then_inc(gt_act.sem, 1)
            step(act, gt_vec, 0, "copied")
            act.activation(sm[:, 0], bt[:, :, 0:8], ACT.Exp, scale=-1.0).then_inc(gt_act.sem, 1)
            step(act, gt_vec, 0, "nabs")
            act.activation(sm[:, 5], sm[:, 4], ACT.Exp).then_inc(gt_act.sem, 1)
            step(act, gt_act, 0, "eabs")
            act.activation(sm[:, 5], sm[:, 5], ACT.Ln, bias=1.0).then_inc(gt_act.sem, 1)

            def first_tap1(n, par, part):
                act.wait_ge(fetched, n + 1)
                act.wait_ge(taken, E_IN1 + part + 1 + 4 * n)
                step(act, pr_pe, n - 2, "turnV")
                step(act, pr_pool, n - 2, "qd")
                act.activation(qkv[:, par, part, :], u[:, part, 0:T], ACT.Copy,
                               scale=hp[:, par, H_TAP + 4 * part:H_TAP + 4 * part + 1]
                               ).then_inc(tap0.sem, 1)

            def prep(ins):
                ins.then_inc(pr_act.sem, 1)

            def prep_squares(n, par):
                step(act, silu, n, "k")
                step(act, pr_vec, n - 1, "qn")
                for part in range(2):
                    prep(act.activation(nsq[:, part, :], qkv[:, par, part, :], ACT.Square))

            def prep_norms(n):
                for part, name in ((0, "q"), (1, "k")):
                    step(act, pr_pe, n, "sum" + name)
                    prep(act.activation(nrs[:, part, :], bank[5 - part][:], ACT.Ln, bias=eps_col))
                    step(act, pr_act, n, "ln" + name)
                    prep(act.activation(nrs[:, part, :], nrs[:, part, :], ACT.Exp, scale=-0.5))

            def prep_decays(n):
                step(act, pr_vec, n, "d3")
                step(act, pr_pool, n - 1, "qd")
                step(act, pr_vec, n - 1, "dec")
                prep(act.activation(eR[:], bank[4][:], ACT.Exp))
                step(act, pr_vec, n, "gap")
                prep(act.activation(flat(gam[:]), flat(gam[:]), ACT.Exp))

            def scan_square(n):
                step(act, sc_pe, n, "o3")
                step(act, sc_pe, n - 1, "sum")
                act.activation(osq, bank[7][:], ACT.Square).then_inc(sc_act.sem, 1)

            def scan_norm(n):
                step(act, sc_pe, n, "sum")
                step(act, sc_vec, n - 1, "out")
                act.activation(ors[:], bank[6][:], ACT.Ln, bias=eps_col,
                               scale=1.0 / P).then_inc(sc_act.sem, 1)
                step(act, sc_act, n, "log")
                act.activation(ors[:], ors[:], ACT.Exp, scale=-0.5).then_inc(sc_act.sem, 1)

            def period(n, par, rounds, proj_, prep_, inv, scan_):
                other = 1 - par
                if prep_:
                    prep_norms(n - 1)
                if proj_:
                    split(U_IN1 + 2, n)
                    first_tap1(n, par, 0)
                if prep_:
                    prep_decays(n - 1)
                if proj_:
                    split(U_IN1 + 3, n)
                    first_tap1(n, par, 1)
                if proj_:
                    split(U_IN1 + 4, n)
                    first_tap1(n, par, 2)
                if scan_:
                    scan_square(n - 3)
                    scan_norm(n - 3)
                if proj_ or prep_:
                    silu_table()
                    if isinstance(n, int) and n == 0:
                        act.nop().then_inc(silu.sem, 1)
                    else:
                        act.wait_ge(taken, E_IN1 + 4 * n)
                        z = dno[:, bass.ds(n - 1, 1), :].rearrange("p a n -> p (a n)")
                        act.activation(z, z, ACT.Silu).then_inc(silu.sem, 1)
                    if proj_:
                        for part, name in enumerate("qkv"):
                            step(act, taps, n, name + "3")
                            act.activation(qkv[:, par, part, :], qkv[:, par, part, :],
                                           ACT.Silu).then_inc(silu.sem, 1)
                            if name == "k":
                                prep_squares(n, par)
                        split(U_IN1 + 5, n)
                    exp_table()
                for k in {8: range(6), 9: (6,), 10: (7,)}.get(n if isinstance(n, int) else 0, ()):
                    act.wait_ge(passes, U_OUT1)
                    step(act, sc_vec, k, "out")
                    fill_from(dno, k)

            all_periods(act, period)
            out_project(U_OUT1, E_OUT1, 3)
            ffn(U_GU1, E_GU1, U_DOWN1, E_DOWN1, 11, None)
            act.wait_ge(out_done, 16 * KT)

        @block.gpsimd
        def _(pool):
            def add_squares(z):
                many(pool, norm_sum, z)
                pool.memset(sqsum[:], 0.0).then_inc(added.sem, 1)

            def add_square(z, m, m_abs):
                pool.wait_ge(squared, 8 * z + m_abs + 1)
                pool.wait_ge(added.sem, 9 * z + 1 + m_abs)
                pool.tensor_tensor(sqsum[:], sqsum[:], sq[:, m % 2, :], ALU.add).then_inc(added.sem, 1)

            def split(unit0, rounds=0):
                pool.wait_ge(w_hi_ready, unit0 + 1 + RING * rounds)
                n = unit_tiles(unit0) * UW
                pool.tensor_tensor(w_lo[:, unit0 % 2, 0:n], raw[:, unit0 % RING, 0:n],
                                   w_hi[:, unit0 % 2, 0:n].bitcast(F32),
                                   ALU.subtract).then_inc(w_lo_ready, 1)

            split(0)
            add_squares(0)
            for m in range(KT):
                add_square(0, m, m)
            split(1)

            def head_cos(n):
                pool.wait_ge(hd_gain, n + 1)
                step(pool, hd_rope, n - 2, "sum")
                pool.tensor_tensor(rope_c[:, n % 2, :], qk[:, n, :], c_(C0_COS, 0, T),
                                   ALU.mult).then_inc(hd_cos, 1)

            def conv_scale(c):
                step(pool, cc_vec, c, "tap2")
                pool.tensor_tensor(conv0[:, c % 2, :], conv0[:, c % 2, :], rstd[:],
                                   ALU.mult).then_inc(cc_scale, 1)

            def divide(n):
                r = n % 2
                step(pool, sm_den, n, "recip")
                pool.tensor_tensor(prob[:, r], prob[:, r], along(rden[:, r, :]), ALU.mult).then_inc(sm_div, 1)

            pool.wait_ge(cst_loaded, 16)
            for n in range(18):
                split(n + 2)
                if 2 <= n <= 6:
                    head_cos(n - 2)
                if 9 <= n <= 16:
                    divide(n - 9)
                if n in (8, 9, 14, 15):
                    conv_scale(n - 8 if n < 10 else n - 12)

            def out_project(u0, z):
                add_squares(z)
                for m in range(KT):
                    split(u0 + m + 2)
                    add_square(z, m, m)

            def ffn(u_gu, u_down, nz):
                def down_(unit0, rounds, m_at):
                    for m in range(2):
                        for half in range(2):
                            if unit0 + 2 * m + half + 2 < U_END:
                                split(unit0 + 2 * m + half + 2, rounds)
                        if nz is not None:
                            add_square(nz, m, m_at + m)

                for t in range(4):
                    split(u_gu + t + 2)
                if nz is not None:
                    add_squares(nz)
                with pool.Fori(0, 9) as i:
                    for t in range(4):
                        split(u_gu + 4 + t + 2, i)
                for t in range(4):
                    split(u_gu + 40 + t + 2)
                with pool.Fori(0, 3) as i:
                    down_(u_down, i, 2 * i)
                down_(u_down + 12, 0, 6)

            out_project(U_OUT0, 1)
            ffn(U_GU0, U_DOWN0, 2)

            def prep(ins):
                ins.then_inc(pr_pool.sem, 1)

            def prep_masks(n):
                step(pool, pr_act, n, "gam")
                step(pool, pr_vec, n - 1, "att")
                prep(pool.tensor_tensor(gamL[:], gam[:], over_chunks(lower[1]), ALU.mult))
                step(pool, pr_pool, n, "gamL")
                prep(pool.tensor_tensor(gamU[:], gam[:], over_chunks(upper[1]), ALU.mult))

            def prep_mt(n, par):
                step(pool, pr_vec, n, "W")
                step(pool, iv_vec, n - 2, "XA")
                prep(pool.tensor_tensor(MT[:, par], W[:, par], over_chunks(c_(C1_PAIR, 1), 2), ALU.mult))
                step(pool, pr_pool, n, "m")
                prep(pool.tensor_tensor(MT[:, par], MT[:, par], over_chunks(ident[1], 2), ALU.add))
                step(pool, pr_pool, n, "MT")
                prep(pool.tensor_tensor(V[:, par], MT[:, par], over_chunks(c_(C1_DIAG, 1), 2), ALU.mult))

            def prep_decayed(n, par):
                step(pool, pr_vec, n, "qn")
                step(pool, pr_act, n, "eR")
                step(pool, sc_pe, n - 2, "o3")
                prep(pool.tensor_tensor(kd[:, par, :], qkv[:, par, 1, :], eR[:], ALU.mult))
                prep(pool.tensor_tensor(qd[:, par, :], qkv[:, par, 0, :], eR[:], ALU.mult))

            def period(n, par, rounds, proj_, prep_, inv, scan_):
                other = 1 - par
                if proj_:
                    split(U_IN1 + 2, n)
                if prep_:
                    prep_masks(n - 1)
                if proj_:
                    split(U_IN1 + 3, n)
                if prep_:
                    prep_mt(n - 1, other)
                if proj_:
                    split(U_IN1 + 4, n)
                if prep_:
                    prep_decayed(n - 1, other)
                if proj_:
                    split(U_IN1 + 5, n)

            all_periods(pool, period)
            out_project(U_OUT1, 3)
            ffn(U_GU1, U_DOWN1, None)


def unit_tiles(unit):
    return FH if U_DOWN0 <= unit < U_IN1 or U_DOWN1 <= unit else KT


MIX_ORDER = [4, 5, 6, 7, 0, 1, 2, 3]

INV_Y = (0, 2, 5, 8, 10, 13)
INV_Z = (1, 4, 7, 9, 12, 15)
SCAN_V = (0, 4, 7, 10)
SCAN_O = (1, 5, 8, 11)
SCAN_K = (3, 6, 9)
TAPS = {5: (0, 1), 6: (0, 2), 7: (0, 3), 8: (1, 1), 9: (1, 2), 10: (1, 3), 12: (2, 1), 13: (2, 2), 14: (2, 3)}


def all_periods(eng, period):
    period(0, 0, 0, True, False, False, False)
    period(1, 1, 0, True, True, False, False)
    period(2, 0, 1, True, True, True, False)
    period(3, 1, 1, True, True, True, True)
    with eng.Fori(0, 2) as i:
        period(2 * i + 4, 0, i + 2, True, True, True, True)
        period(2 * i + 5, 1, i + 2, True, True, True, True)
    period(8, 0, 0, False, True, True, True)
    period(9, 1, 0, False, False, True, True)
    period(10, 0, 0, False, False, False, True)


def constants():
    f = np.float32
    i = np.arange(P)
    kept = np.zeros((P, K_N), f)
    kept[:, K_ONES:K_ONES + P] = 1
    kept[:, K_EPS] = EPS
    c0 = np.zeros((P, C0_N), f)
    c1 = np.zeros((P, C1_N), f)
    for c in (c0, c1):
        c[:, C_ID:C_ID + P] = np.eye(P)
        c[:, C_UP:C_UP + P] = i[:, None] <= i[None]
        c[:, C_LOW:C_LOW + P] = i[:, None] > i[None]
    c0[:, C0_HALF:C0_HALF + P] = (i[:, None] // HEAD) == (i[None] // HEAD)
    for m in range(P):
        if m % HEAD < HEAD // 2:
            c0[m + HEAD // 2, C0_ROT + m] = -1
        else:
            c0[m - HEAD // 2, C0_ROT + m] = 1
    c0[:, C0_SUP:C0_SUP + P] = i[:, None] < i[None]
    inv_freq = f(10000.0) ** (-np.arange(0, HEAD, 2, dtype=f) / f(HEAD))
    ang = np.arange(T, dtype=f)[None] * inv_freq[i % (HEAD // 2)][:, None]
    c0[:, C0_COS:C0_COS + T] = np.cos(ang)
    c0[:, C0_SIN:C0_SIN + T] = np.sin(ang)
    c0[:, C0_NEG] = NEG
    row, col = i[:, None], i[None]
    c1[:, C1_PAIR:C1_PAIR + P] = row ^ 1 == col
    for lvl in range(1, 7):
        s = 1 << lvl
        even = row // s % 2 == 0
        same = row // s == col // s
        at = P * (lvl - 1)
        c1[:, C1_OFF + at:C1_OFF + at + P] = row // s ^ 1 == col // s
        c1[:, C1_DIAG + at:C1_DIAG + at + P] = same & np.where(even, row >= col, row <= col)
    return kept, c0, c1


def units(w, kt):
    n = w.shape[1] // UW
    return np.ascontiguousarray(w.reshape(kt, P, n, UW).transpose(2, 1, 0, 3)).reshape(n, P, kt * UW)


def kernel(**inputs):
    import concourse.bacc as bacc
    from concourse.bass_utils import run_bass_kernel_spmd as run

    a = {k: np.asarray(v) for k, v in inputs.items()}
    cols = lambda v: v.reshape(-1, P).T
    rows = lambda v: np.broadcast_to(v.reshape(1, -1), (P, v.size))

    heads = [h for t in range(4) for h in (t, t + 4)]
    w = a["even_w_in"][0]
    w_q = w[:, 0:512].reshape(D, 8, HEAD)[:, heads].reshape(D, 512)
    w_kv = w[:, 512:768]
    gate_b, gate_c, xin = w[:, 768:1280], w[:, 1280:1792], w[:, 1792:2304]
    w_in0 = np.concatenate([w_q, w_kv] + [m[:, 2 * P * g:2 * P * (g + 1)] for g in range(2)
                                          for m in (gate_c, xin, gate_b)], 1)
    wo = a["even_w_out"][0]
    w_out0 = np.concatenate([wo[0:512].reshape(8, HEAD, D)[heads].reshape(512, D), wo[512:]], 0)
    w1 = a["odd_w_in"][0]
    w_in1 = w1[:, 0:4 * D].reshape(D, 4, DN_HEADS, P).transpose(0, 2, 1, 3).reshape(D, 4 * D)

    def gate_up(m):
        g, u = (h.reshape(D, -1, 1, 2 * P) for h in (m[:, :FF], m[:, FF:]))
        return np.concatenate([g, u], 2).reshape(D, 2 * FF)

    def down(m):
        return np.ascontiguousarray(m.reshape(2, FH, P, KT, UW).transpose(3, 0, 2, 1, 4)
                                    ).reshape(DOWN_UNITS, P, FH * UW)

    params = np.concatenate([
        cols(a["even_norm"][0]), cols(a["ffn_norm"][0]), cols(a["odd_norm"][0]), cols(a["ffn_norm"][1]),
        np.tile(a["even_q_gain"][0], 2)[:, None], np.tile(a["even_k_gain"][0], 2)[:, None],
        rows(a["even_sinks"][0]),
        a["even_conv_w"][0].reshape(3, 4, P).transpose(2, 1, 0).reshape(P, 12),
        rows(a["odd_a_log"][0]), rows(a["odd_dt_bias"][0]), a["odd_o_gain"][0][:, None],
        a["odd_conv_w"][0].reshape(4, 3, DN_HEADS, P).transpose(3, 2, 1, 0).reshape(P, 96),
        w1[:, 4 * D:].reshape(KT, P, 16).transpose(1, 0, 2).reshape(P, 128),
    ], 1)
    kept, consts0, consts1 = constants()
    arrays = {
        "xT": a["x"][0].T.reshape(KT, P, T).transpose(1, 0, 2).reshape(P, KT * T),
        "params": params,
        "kept": kept, "consts0": consts0, "consts1": consts1,
        "w_in0": units(w_in0, KT), "w_out0": units(w_out0, KT),
        "w_gu0": units(gate_up(a["ffn_w_gate_up"][0]), KT), "w_down0": down(a["ffn_w_down"][0]),
        "w_in1": units(w_in1, KT), "w_out1": units(a["odd_w_out"][0], KT),
        "w_gu1": units(gate_up(a["ffn_w_gate_up"][1]), KT), "w_down1": down(a["ffn_w_down"][1]),
    }
    nc = bacc.Bacc("TRN2", target_bir_lowering=False, num_devices=1)
    aps = []
    for name, v in arrays.items():
        arrays[name] = np.ascontiguousarray(v)
        aps.append(nc.dram_tensor(name, v.shape, F32, kind="ExternalInput").ap())
    outT = nc.dram_tensor("outT", (KT, P, T), F32, kind="ExternalOutput").ap()
    trunk(nc, *aps, outT)
    r = run(nc, [arrays], core_ids=[0])
    return np.ascontiguousarray(r.results[0]["outT"].reshape(D, T).T).reshape(1, T, D)
```

```python
from contextlib import ExitStack

import numpy as np

import concourse.bass as bass
from concourse import mybir

F32 = mybir.dt.float32
F32R = mybir.dt.float32r
U32 = mybir.dt.uint32
ALU = mybir.AluOpType
ACT = mybir.ActivationFunctionType
AX = mybir.AxisListType

P = 128
T = 512
D = 1024
KT = D // P
DN_HEADS = 8
HEAD = 64
NB = T // P
FF = 2816
FT = FF // P
FH = FT // 2
UW = P
EPS = 1e-6
RING = 4
SLOT = FH * UW
NEG = -1e30

IN0_UNITS, OUT_UNITS, GU_UNITS, DOWN_UNITS, IN1_UNITS, LATE_UNITS = 18, 8, 44, 16, 32, 4
EARLY = 5
LATE = DN_HEADS - EARLY
U_IN0 = 0
U_OUT0 = U_IN0 + IN0_UNITS
U_GU0 = U_OUT0 + OUT_UNITS
U_DOWN0 = U_GU0 + GU_UNITS
U_IN1 = U_DOWN0 + DOWN_UNITS
U_OUT1 = U_IN1 + IN1_UNITS
U_LATE = U_OUT1 + OUT_UNITS
U_GU1 = U_LATE + LATE_UNITS
U_DOWN1 = U_GU1 + GU_UNITS
U_END = U_DOWN1 + DOWN_UNITS
E_IN0 = 0
E_OUT0 = E_IN0 + 18
E_GU0 = E_OUT0 + 8
E_DOWN0 = E_GU0 + 44
E_IN1 = E_DOWN0 + 8
E_OUT1 = E_IN1 + 32
E_LATE = E_OUT1 + 8
E_GU1 = E_LATE + 8
E_DOWN1 = E_GU1 + 44

K_ONES, K_EPS, K_N = 0, P, P + 1
C_ID, C_UP, C_LOW = 0, P, 2 * P
C0_HALF, C0_ROT, C0_SUP = 3 * P, 4 * P, 5 * P
C0_COS = 6 * P
C0_SIN = C0_COS + T
C0_NEG = C0_SIN + T
C0_N = C0_NEG + 1
C1_PAIR, C1_PAIR_V = 3 * P, 4 * P
C1_OFF, C1_DIAG = 5 * P, 11 * P
C1_N = 17 * P
R_GAIN = 0
R_QG = 32
R_KG = 33
R_SINK = 34
R_CONV0 = 42
R_ALOG = 54
R_DT = 62
R_OG = 70
R_HEAD = 71
R_BA = R_HEAD + 96
R_N = R_BA + 128
H_TAP, H_G, H_GC, H_BETA, H_NBETA, H_N = 0, 12, 16, 20, 24, 28


class Steps:

    def __init__(self, sem, names):
        self.sem = sem
        self.names = names.split()

    def after(self, n, step):
        return n * len(self.names) + self.names.index(step) + 1


def trunk(nc, xT, params, kept, consts0, consts1, w_in0, w_out0, w_gu0, w_down0, w_in1, w_early1,
          w_late1, w_gu1, w_down1, outT):
    with ExitStack() as ctx:
        def sb(name, shape, dt=F32):
            return ctx.enter_context(nc.sbuf_tensor(name, shape, dt))

        def sem(name):
            return ctx.enter_context(nc.semaphore(name))

        x = sb("x", [P, KT, T])
        mov_hi = sb("mov_hi", [P, KT, T], F32R)
        mov_lo = sb("mov_lo", [P, KT, T], F32R)
        raw = sb("raw", [P, RING, SLOT])
        w_hi = sb("w_hi", [P, 2, SLOT], F32R)
        w_lo = sb("w_lo", [P, 2, SLOT], F32R)
        kpt = sb("kpt", [P, K_N])
        prm = sb("prm", [P, R_N])
        rstd = sb("rstd", [P, T])
        sq = sb("sq", [P, 4, T])
        sqsum = sb("sqsum", [P, T])

        l0 = ExitStack()

        def sb0(name, shape, dt=F32):
            return l0.enter_context(nc.sbuf_tensor(name, shape, dt))

        cst0 = sb0("cst0", [P, C0_N])
        qk = sb0("qk", [P, 5, T])
        vT = sb0("vT", [P, T])
        rstd2 = sb0("rstd2", [P, T])
        vtok = sb0("vtok", [P, NB, P])
        hsq = sb0("hsq", [P, 2, T])
        hrs = sb0("hrs", [P, 2, T])
        rope_c = sb0("rope_c", [P, 2, T])
        rope_s = sb0("rope_s", [P, T])
        gate_c = sb0("gate_c", [P, 2, T])
        cx = sb0("cx", [P, 2, T + 2])
        conv0 = sb0("conv0", [P, 2, T])
        prob = sb0("prob", [P, 2, 4, P])
        probT = sb0("probT", [P, 2, 2, 4, P])
        mx = sb0("mx", [P, 2, 4])
        nmx = sb0("nmx", [P, 2, 4])
        sgap = sb0("sgap", [P, 2, 4])
        esink = sb0("esink", [P, 2, 4])
        den = sb0("den", [P, 2, 4])
        den2 = sb0("den2", [P, 2, 4])
        rden = sb0("rden", [P, 2, 4])
        nsink = sb0("nsink", [P, 8])
        mix = sb0("mix", [P, KT, T])
        l0.close()
        lf = ExitStack()
        act_hi = lf.enter_context(nc.sbuf_tensor("act_hi", [P, FT, T], F32R))
        act_lo = lf.enter_context(nc.sbuf_tensor("act_lo", [P, FT, T], F32R))
        gs = lf.enter_context(nc.sbuf_tensor("gs", [P, 2, T], F32))
        us = lf.enter_context(nc.sbuf_tensor("us", [P, 2, T], F32))
        lf.close()
        cst1 = sb("cst1", [P, C1_N])
        u = sb("u", [P, 3, T + 3])
        qkv = sb("qkv", [P, 2, 3, T])
        nsq = sq[:, 2:4, :]
        nrs = nsq
        nsq_hi = sb("nsq_hi", [P, 2, T], F32R)
        nsq_lo = sb("nsq_lo", [P, 2, T], F32R)
        ones_r = sb("ones_r", [P, P], F32R)
        eR = sb("eR", [P, T])
        gam = sb("gam", [P, NB, P])
        gamL = sb("gamL", [P, NB, P])
        gamU = gam
        kd = sb("kd", [P, 2, T])
        qd = sb("qd", [P, 2, T])
        attT = sb("attT", [P, 2, NB, P])
        kdec = sb("kdec", [P, 2, NB, P])
        bv = sb("bv", [P, 2, NB, P])
        nA = sb("nA", [P, NB, P])
        W = sb("W", [P, 2, 2, P])
        WT = sb("WT", [P, 2, P])
        M = sb("M", [P, 2, 2, P])
        R = sb("R", [P, 2, 2, P])
        V = sb("V", [P, 2, 2, P])
        Y = sb("Y", [P, 2, P])
        XT = sb("XT", [P, 2, NB, P])
        S = sb("S", [P, P])
        R1 = sb("R1", [P, P])
        vn = sb("vn", [P, P])
        hp = sb("hp", [P, 2, H_N])
        decb = sb("decb", [P, 2, NB])
        betab = sb("betab", [P, 2, NB])
        HP = sb("HP", [P, DN_HEADS, H_N])
        ors = sb("ors", [P, T])
        osq, og = sq[:, 0, :], sq[:, 1, :]
        dno = sb("dno", [P, KT, T])
        ba = gam[0:16].rearrange("p c n -> p (c n)")
        bt = sb("bt", [P, NB, 16])
        esum = sb("esum", [P, 8])
        sm = sb("sm", [P, 8, NB, 8])

        bank = [ctx.enter_context(nc.psum_tensor(f"bank{i}", [P, T], F32)) for i in range(8)]

        def c_(at, layer=0, n=P):
            return (cst0, cst1)[layer][:, at:at + n]

        ones, eps_col = kpt[:, K_ONES:K_ONES + P], kpt[:, K_EPS:K_EPS + 1]
        ident = [c_(C_ID, n) for n in range(2)]
        upper = [c_(C_UP, n) for n in range(2)]
        lower = [c_(C_LOW, n) for n in range(2)]

        def chunks(ap):
            return ap.rearrange("p (c n) -> p c n", n=P)

        def over_chunks(ap, n=NB):
            return ap.unsqueeze(1).to_broadcast([P, n, ap.shape[1]])

        def along(ap, n=P):
            return ap.unsqueeze(2).to_broadcast([P, ap.shape[1], n])

        x_loaded = [sem(f"x_loaded{i}") for i in range(4)]
        kept_loaded = sem("kept_loaded")
        cst_loaded = sem("cst_loaded")
        prm_loaded = sem("prm_loaded")
        unit_loaded = [sem(f"unit_loaded{i}") for i in range(RING)]
        w_hi_ready = sem("w_hi_ready")
        w_lo_ready = sem("w_lo_ready")
        hi_ready = sem("hi_ready")
        lo_ready = sem("lo_ready")
        passes = sem("passes")
        late_half = sem("late_half")
        taken = sem("taken")
        squared = sem("squared")
        added = Steps(sem("added"), "zero t0 t1 t2 t3 t4 t5 t6 t7")
        norm_sum = sem("norm_sum")
        rstd_log = sem("rstd_log")
        rstd_ready = sem("rstd_ready")
        rstd2_ready = sem("rstd2_ready")
        out_done = sem("out_done")
        hd_sq = sem("hd_sq")
        hd_sum = sem("hd_sum")
        hd_norm = Steps(sem("hd_norm"), "log rsqrt")
        hd_gain = sem("hd_gain")
        hd_rot = sem("hd_rot")
        hd_cos = sem("hd_cos")
        hd_rope = Steps(sem("hd_rope"), "sin sum")
        v_turned = sem("v_turned")
        v_tok = sem("v_tok")
        nsink_ready = sem("nsink_ready")
        scored = sem("scored")
        sm_max = Steps(sem("sm_max"), "join max neg gap")
        sm_exp = Steps(sem("sm_exp"), "e0 e1 e2 e3 sink")
        sm_den = Steps(sem("sm_den"), "sum recip")
        sm_div = sem("sm_div")
        turned = sem("turned")
        sm_mask = Steps(sem("sm_mask"), "cur prev")
        pv_done = sem("pv_done")
        y_copied = sem("y_copied")
        cc_tap = sem("cc_tap")
        cc_vec = Steps(sem("cc_vec"), "tap1 tap2")
        cc_scale = sem("cc_scale")
        pad0 = sem("pad0")
        silu_g = sem("silu_g")
        gated = sem("gated")
        act_hi_ready = sem("act_hi_ready")
        act_lo_ready = sem("act_lo_ready")
        gt_x = sem("gt_x")
        gt_x_used = sem("gt_x_used")
        gt_pe = Steps(sem("gt_pe"), "turned cum")
        gt_vec = Steps(sem("gt_vec"), "scaled copied taps plus1 beta beta_h nbeta_h z nabs relu "
                                      "softplus g g_h gc_h")
        gt_act = Steps(sem("gt_act"), "ea ebeta eabs log")
        zeroed = sem("zeroed")
        ones_ready = sem("ones_ready")
        fetched = sem("fetched")
        tap0 = Steps(sem("tap0"), "q k v")
        taps = Steps(sem("taps"), "q1 q2 q3 k1 k2 k3 v1 v2 v3")
        silu = Steps(sem("silu"), "q k v")
        silu_z = sem("silu_z")
        pr_pe = Steps(sem("pr_pe"), "sumq sumk rows gram turnA qk turnK turnV")
        pr_vec = Steps(sem("pr_vec"), "kn qn d0 d1 d2 d3 gap A0 A1 A2 A3 W WT m M R att kdec bv dec beta")
        pr_act = Steps(sem("pr_act"), "sqq hiq sqk hik lnq rsq lnk rsk eR gam")
        pr_pool = Steps(sem("pr_pool"), "loq lok gamL gamU v V kd qd")
        iv_pe = Steps(sem("iv_pe"), "Y1 Z1 Y2 T1 Z2 Y3 T2 Z3 Y4 T3 Z4 Y5 T4 Z5 Y6 T5 Z6 T6")
        iv_vec = Steps(sem("iv_vec"), "Y1 M1 R1 Y2 V1 M2 R2 Y3 V2 M3 R3 Y4 V3 M4 R4 Y5 V4 M5 R5 Y6 V5 "
                                      "M6 XB XA")
        sc_pe = Steps(sem("sc_pe"), "v0 o0 k1 v1 o1 k2 v2 o2 k3 v3 o3 sum")
        sc_vec = Steps(sem("sc_vec"), "vn0 S0 r1 vn1 S1 r2 vn2 S2 r3 vn3 gain out")
        sc_act = Steps(sem("sc_act"), "sq log rs")

        block = ctx.enter_context(nc.Block())

        def step(eng, of, n, name):
            if not isinstance(n, int) or n >= 0:
                eng.wait_ge(of.sem, of.after(n, name))

        def many(eng, s, n):
            if not isinstance(n, int) or n > 0:
                eng.wait_ge(s, n)

        def pairs(ap):
            return ap.rearrange("p (q n) -> p q n", n=P)

        def flat(ap):
            return ap.rearrange("p c n -> p (c n)")

        @block.sync
        def _(sp):
            def load(unit0, rounds, src, kt):
                if not (isinstance(rounds, int) and unit0 + RING * rounds < RING):
                    sp.wait_ge(w_lo_ready, unit0 - RING + 1 + RING * rounds)
                slot = unit0 % RING
                sp.dma_start(raw[:, slot, 0:kt * UW], src).then_inc(unit_loaded[slot], 16)

            def phase(unit0, w, kt, rounds):
                with sp.Fori(0, rounds) as i:
                    for n in range(RING):
                        load(unit0 + n, i, w[4 * i + n], kt)

            for n in range(IN0_UNITS):
                if n < 4:
                    sp.dma_start(flat(x[:, 2 * n:2 * n + 2, :]), xT[:, 2 * T * n:2 * T * (n + 1)]
                                 ).then_inc(x_loaded[n], 16)
                if n == 2:
                    sp.wait_ge(x_loaded[1], 16)
                load(U_IN0 + n, 0, w_in0[n], KT)
            phase(U_OUT0, w_out0, KT, 2)
            phase(U_GU0, w_gu0, KT, 11)
            phase(U_DOWN0, w_down0, FH, 4)
            phase(U_IN1, w_in1, KT, 8)
            phase(U_OUT1, w_early1, EARLY, 2)
            phase(U_LATE, w_late1, 2 * LATE, 1)
            phase(U_GU1, w_gu1, KT, 11)
            phase(U_DOWN1, w_down1, FH, 4)

        @block.tensor
        def _(pe):
            def unit_ap(w, unit0):
                return w[:, unit0 % 2, :].rearrange("p (k n) -> p k n", n=UW)

            def hi_passes(dst, unit0, src_hi, src_lo, ks, first, each=None):
                w = unit_ap(w_hi, unit0)
                for n, k in enumerate(ks):
                    if each:
                        each(n)
                    pe.matmul(dst, w[:, k, :], src_hi[:, k, :], start=first and n == 0, stop=False)
                    pe.matmul(dst, w[:, k, :], src_lo[:, k, :], start=False, stop=False)

            def lo_passes(dst, unit0, src_hi, ks, last):
                w = unit_ap(w_lo, unit0)
                for n, k in enumerate(ks):
                    mm = pe.matmul(dst, w[:, k, :], src_hi[:, k, :], start=False,
                                   stop=last and n == len(ks) - 1)
                return mm

            def project(dst, unit0, rounds, ks=range(KT), src_hi=mov_hi, src_lo=mov_lo, first=True,
                        last=True, each=None):
                pe.wait_ge(w_hi_ready, unit0 + 1 + RING * rounds)
                hi_passes(dst, unit0, src_hi, src_lo, ks, first, each)
                pe.wait_ge(w_lo_ready, unit0 + 1 + RING * rounds)
                lo_passes(dst, unit0, src_hi, ks, last).then_inc(passes, 1)

            def filled(fill):
                return lambda n: pe.wait_ge(lo_ready, 8 * fill + n + 1)

            def sum_at(z, at):
                return lambda n: sum_squares(z) if n == at else None

            def sum_squares(z):
                step(pe, added, z, "t7")
                pe.matmul(bank[7][:], ones, sqsum[:], start=True, stop=True).then_inc(norm_sum, 1)

            def head_sum(n):
                pe.wait_ge(hd_sq, n + 1)
                step(pe, hd_norm, n - 1, "log")
                pe.matmul(bank[2][:], c_(C0_HALF), hsq[:, n % 2, :], start=True,
                          stop=True).then_inc(hd_sum, 1)

            def head_rot(n):
                pe.wait_ge(hd_gain, n + 1)
                step(pe, hd_rope, n - 1, "sin")
                pe.matmul(bank[3][:], c_(C0_ROT), qk[:, n, :], start=True, stop=True).then_inc(hd_rot, 1)

            def turn_v():
                pe.wait_ge(taken, E_IN0 + 6)
                pe.wait_ge(rstd_ready, 1)
                for b in range(NB):
                    mm = pe.transpose(bank[7][:, b * P:(b + 1) * P], vT[:, b * P:(b + 1) * P], ident[0])
                mm.then_inc(v_turned, 1)

            def scores(n):
                b, g = divmod(n, 2)
                step(pe, hd_rope, 4, "sum")
                step(pe, sm_max, n - 1, "join")
                step(pe, sm_exp, n - 2, "e3")
                rows = slice(g * HEAD, (g + 1) * HEAD)
                for t in range(4):
                    q = qk[rows, t, b * P:(b + 1) * P]
                    if b:
                        pe.matmul(bank[4][:, t * P:(t + 1) * P], q, qk[rows, 4, (b - 1) * P:b * P],
                                  start=True, stop=True)
                    mm = pe.matmul(bank[5 + g][:, t * P:(t + 1) * P], q, qk[rows, 4, b * P:(b + 1) * P],
                                   start=True, stop=True)
                mm.then_inc(scored, 1)

            def turn_probs(n):
                pe.wait_ge(sm_div, n + 1)
                pe.wait_ge(v_tok, 1)
                step(pe, sm_mask, n - 1, "prev")
                for t in range(4):
                    mm = pe.transpose(bank[7][:, t * P:(t + 1) * P], prob[:, n % 2, t, :], ident[0])
                mm.then_inc(turned, 1)

            def pv(n):
                b, g = divmod(n, 2)
                step(pe, sm_mask, n, "prev")
                many(pe, y_copied, b - 1)
                rows = slice(g * HEAD, (g + 1) * HEAD)
                y = bank[2 + b % 2]
                for t in range(4):
                    if b:
                        pe.matmul(y[rows, t * P:(t + 1) * P], vtok[:, b - 1, rows],
                                  probT[:, n % 2, 0, t, :], start=True, stop=False)
                    mm = pe.matmul(y[rows, t * P:(t + 1) * P], vtok[:, b, rows],
                                   probT[:, n % 2, 1, t, :], start=b == 0, stop=True)
                mm.then_inc(pv_done, 1)

            for n in range(IN0_UNITS):
                if n == 1:
                    pe.wait_ge(kept_loaded, 16)
                many(pe, taken, n - 1)
                project(bank[n % 2][:], U_IN0 + n, 0, each=(filled(0), sum_at(0, 3))[n] if n < 2 else None)
                if n == 2:
                    pe.wait_ge(cst_loaded, 16)
                if 2 <= n <= 6:
                    head_sum(n - 2)
                if 3 <= n <= 7:
                    head_rot(n - 3)
                if n == 7:
                    turn_v()
                if 8 <= n < 16:
                    scores(n - 8)
                if 10 <= n:
                    turn_probs(n - 10)
                if 11 <= n:
                    pv(n - 11)
            pv(7)

            def out_project(u0, e0, fill, order):
                for m in range(KT):
                    pe.wait_ge(taken, e0 + max(m - 1, 0))
                    project(bank[m % 2][:], u0 + m, 0, ks=order, each=filled(fill) if m == 0 else None)

            out_project(U_OUT0, E_OUT0, 1, MIX_ORDER)

            def ffn(u_gu, e_gu, u_down, e_down, z, fill, blk0):
                def gate_up(unit0, rounds, e_at, first=False):
                    for t in range(4):
                        if not first:
                            pe.wait_ge(taken, e_at + t + 1)
                        elif t < 2:
                            pe.wait_ge(taken, e_gu - 1 + t)
                        project(bank[t][:], unit0 + t, rounds,
                                each=(filled(fill), sum_at(z, 4), None, None)[t] if first else None)

                gate_up(u_gu, 0, None, first=True)
                with pe.Fori(0, 10) as i:
                    gate_up(u_gu + 4, i, e_gu + 4 * i)
                with pe.Fori(0, 4) as i:
                    for m in range(2):
                        for half in range(2):
                            if half == 0:
                                pe.wait_ge(taken, e_down + m - 1 + 2 * i)
                            if m == 0:
                                pe.wait_ge(act_lo_ready, 2 * blk0 + FH * (1 + half))
                            part = slice(half * FH, (half + 1) * FH)
                            project(bank[m][:], u_down + 2 * m + half, i, range(FH),
                                    act_hi[:, part, :], act_lo[:, part, :],
                                    first=half == 0, last=half == 1)

            ffn(U_GU0, E_GU0, U_DOWN0, E_DOWN0, 1, 2, 0)

            def gate_project():
                pe.wait_ge(prm_loaded, 16)
                for k in range(KT):
                    pe.wait_ge(gt_x, k + 1)
                    pe.matmul(bank[6][0:16, :], prm[:, R_BA + 16 * k:R_BA + 16 * (k + 1)],
                              (gam, gamL)[k % 2][:].rearrange("p c n -> p (c n)"), start=k == 0,
                              stop=k == KT - 1).then_inc(gt_x_used, 1)
                sum_squares(2)

            def gate_turn():
                pe.wait_ge(cst_loaded, 32)
                step(pe, gt_vec, 0, "scaled")
                for c in range(NB):
                    mm = pe.transpose(bank[5][:, 16 * c:16 * (c + 1)], ba[:, c * P:(c + 1) * P],
                                      cst1[0:16, C_ID:C_ID + 16])
                mm.then_inc(gt_pe.sem, 1)

            def gate_cumsum():
                step(pe, gt_vec, 0, "g")
                pe.matmul(bank[6][:, 0:32], upper[1], flat(sm[:, 6]), start=True,
                          stop=True).then_inc(gt_pe.sem, 1)

            def project_quarter(n, j):
                tile, part = divmod(j, 4)
                dst = bank[tile % 2][:]
                if part == 0:
                    if not isinstance(n, int) or n or tile != 1:
                        pe.wait_ge(taken, E_IN1 - 1 + tile + 4 * n)
                    pe.wait_ge(w_hi_ready, U_IN1 + tile + 1 + 4 * n)
                if part < 3:
                    ks = (range(0, 3), range(3, 6), range(6, 8))[part]
                    hi_passes(dst, U_IN1 + tile, mov_hi, mov_lo, ks, first=part == 0,
                              each=(lambda _, k0=ks[0]: pe.wait_ge(lo_ready, 8 * 3 + k0 + len(ks)))
                              if isinstance(n, int) and n == 0 and tile == 0 else None)
                else:
                    pe.wait_ge(w_lo_ready, U_IN1 + tile + 1 + 4 * n)
                    lo_passes(dst, U_IN1 + tile, mov_hi, range(KT), last=True).then_inc(passes, 1)

            def prep_sums(n):
                pe.wait_ge(ones_ready, 1)
                step(pe, pr_vec, n - 1, "bv")
                for part, name in enumerate("qk"):
                    step(pe, pr_pool, n, "lo" + name)
                    dst = bank[5 - part][:]
                    pe.matmul(dst, ones_r[:], nsq_hi[:, part, :], start=True, stop=False)
                    pe.matmul(dst, ones_r[:], nsq_lo[:, part, :], start=False,
                              stop=True).then_inc(pr_pe.sem, 1)

            def prep_rows(n, par):
                step(pe, pr_act, n, "lnk")
                for c in range(NB):
                    mm = pe.matmul(bank[4][:, c * P:(c + 1) * P],
                                   hp[:, par, H_G + c:H_G + c + 1].to_broadcast([P, P]), upper[1],
                                   start=True, stop=True)
                mm.then_inc(pr_pe.sem, 1)

            def prep_gram(n, par):
                step(pe, pr_vec, n, "kn")
                for c in range(NB):
                    kc = qkv[:, par, 1, c * P:(c + 1) * P]
                    mm = pe.matmul(bank[5][:, c * P:(c + 1) * P], kc, kc, start=True, stop=True)
                mm.then_inc(pr_pe.sem, 1)

            def prep_turn_a(n):
                step(pe, pr_vec, n, "A3")
                for c in range(NB):
                    mm = pe.transpose(bank[5][:, c * P:(c + 1) * P], nA[:, c, :], ident[1])
                mm.then_inc(pr_pe.sem, 1)

            def prep_qk(n, par):
                step(pe, pr_act, n, "eR")
                step(pe, pr_vec, n, "qn")
                for c in range(NB):
                    mm = pe.matmul(bank[4][:, c * P:(c + 1) * P], qkv[:, par, 1, c * P:(c + 1) * P],
                                   qkv[:, par, 0, c * P:(c + 1) * P], start=True, stop=True)
                mm.then_inc(pr_pe.sem, 1)

            def prep_turn_kv(n, par, part):
                step(pe, pr_vec, n, "WT" if part == 1 else "att")
                dst = bank[5] if part == 1 else bank[4]
                for c in range(NB):
                    mm = pe.transpose(dst[:, c * P:(c + 1) * P], qkv[:, par, part, c * P:(c + 1) * P],
                                      ident[1])
                mm.then_inc(pr_pe.sem, 1)

            def inv_y(n, par, lvl):
                if lvl == 1:
                    step(pe, pr_vec, n, "R")
                    step(pe, iv_vec, n - 1, "M6")
                else:
                    step(pe, iv_vec, n, f"R{lvl - 1}")
                for q in range(2):
                    mm = pe.matmul(bank[2][:, q * P:(q + 1) * P], W[:, par, q, :], R[:, par, q, :],
                                   start=True, stop=True)
                mm.then_inc(iv_pe.sem, 1)

            def inv_z(n, par, lvl):
                step(pe, iv_vec, n, f"Y{lvl}")
                if lvl == 1:
                    step(pe, pr_pool, n, "V")
                else:
                    step(pe, iv_vec, n, f"V{lvl - 1}")
                for q in range(2):
                    mm = pe.matmul(bank[2][:, (q + 2) * P:(q + 3) * P], V[:, par, q, :], Y[:, q, :],
                                   start=True, stop=True)
                mm.then_inc(iv_pe.sem, 1)

            def inv_t(n, par, lvl):
                step(pe, iv_vec, n, f"M{lvl}")
                if lvl == 1:
                    step(pe, iv_vec, n - 1, "XA")
                for q in range(2):
                    mm = pe.transpose(bank[3][:, q * P:(q + 1) * P], M[:, par, q, :], ident[1])
                mm.then_inc(iv_pe.sem, 1)

            def scan_k(n, par, c):
                step(pe, sc_vec, n, f"S{c - 1}")
                pe.matmul(bank[6][:, 0:P], kd[:, par, c * P:(c + 1) * P], S[:], start=True,
                          stop=True).then_inc(sc_pe.sem, 1)

            def scan_v(n, par, c):
                if c == 0:
                    step(pe, iv_vec, n, "XA")
                    step(pe, sc_act, n - 1, "log")
                    rhs = bv[:, par, 0, :]
                else:
                    step(pe, sc_vec, n, f"r{c}")
                    rhs = R1[:]
                pe.matmul(bank[6][:, P:2 * P], XT[:, par, c, :], rhs, start=True,
                          stop=True).then_inc(sc_pe.sem, 1)

            def scan_o(n, par, c):
                if c == 0:
                    step(pe, sc_vec, n - 1, "gain")
                    step(pe, pr_pool, n, "qd")
                step(pe, sc_vec, n, f"vn{c}")
                o = bank[7][:, c * P:(c + 1) * P]
                if c:
                    pe.matmul(o, S[:], qd[:, par, c * P:(c + 1) * P], start=True, stop=False)
                mm = pe.matmul(o, vn[:], attT[:, par, c, :], start=c == 0, stop=True)
                if c < NB - 1:
                    mm = pe.matmul(bank[6][:, 2 * P:3 * P], kdec[:, par, c, :], vn[:], start=True,
                                   stop=True)
                mm.then_inc(sc_pe.sem, 1)

            def scan_sum(n):
                step(pe, sc_act, n, "sq")
                pe.matmul(bank[6][:], ones, osq, start=True, stop=True).then_inc(sc_pe.sem, 1)

            def early_piece(m, piece):
                hi_ks, lo_ks = EARLY_PIECES[piece]
                dst = bank[m % 2][:]
                if piece == 0:
                    if m == 0:
                        pe.wait_ge(lo_ready, 8 * 4 + EARLY)
                    pe.wait_ge(taken, E_OUT1 + max(m - 1, 0))
                    pe.wait_ge(w_hi_ready, U_OUT1 + m + 1)
                if hi_ks:
                    hi_passes(dst, U_OUT1 + m, mov_hi, mov_lo, hi_ks, first=piece == 0)
                if lo_ks:
                    pe.wait_ge(w_lo_ready, U_OUT1 + m + 1)
                    last = lo_ks[-1] == EARLY - 1
                    mm = lo_passes(dst, U_OUT1 + m, mov_hi, lo_ks, last)
                    if last:
                        mm.then_inc(passes, 1)

            def late_project():
                for b in range(LATE_UNITS):
                    unit = U_LATE + b
                    pe.wait_ge(w_hi_ready, unit + 1)
                    for t in range(2):
                        wh, wl = (unit_ap(w, unit)[:, LATE * t:LATE * (t + 1)] for w in (w_hi, w_lo))
                        pe.wait_ge(taken, E_LATE + 2 * b + t - 1)
                        for k in range(LATE):
                            if unit == U_LATE and t == 0:
                                pe.wait_ge(lo_ready, 8 * 4 + EARLY + k + 1)
                            pe.matmul(bank[t][:], wh[:, k, :], mov_hi[:, EARLY + k, :], start=k == 0, stop=False)
                            pe.matmul(bank[t][:], wh[:, k, :], mov_lo[:, EARLY + k, :], start=False, stop=False)
                        if t == 0:
                            pe.wait_ge(w_lo_ready, unit + 1)
                        for k in range(LATE):
                            mm = pe.matmul(bank[t][:], wl[:, k, :], mov_hi[:, EARLY + k, :], start=False,
                                           stop=k == LATE - 1)
                        mm.then_inc((late_half, passes)[t], 1)

            def period(n, par, proj, prep, inv, scan):
                other = 1 - par
                for j in range(16):
                    if proj:
                        project_quarter(n, j)
                        if isinstance(n, int) and n == 0 and j in GATES_AT:
                            (gate_project, gate_turn, gate_cumsum)[GATES_AT.index(j)]()
                    else:
                        for m, piece in EARLY_STEPS.get((n, j), ()):
                            early_piece(m, piece)
                    if prep and j == 1:
                        prep_sums(n - 1)
                    if inv:
                        if j in INV_Y:
                            inv_y(n - 2, par, INV_Y.index(j) + 1)
                        if j in INV_Z:
                            inv_z(n - 2, par, INV_Z.index(j) + 1)
                        if j in INV_T:
                            inv_t(n - 2, par, INV_T.index(j) + 1)
                    if scan:
                        if j in SCAN_K:
                            scan_k(n - 3, other, SCAN_K.index(j) + 1)
                        if j in SCAN_V:
                            scan_v(n - 3, other, SCAN_V.index(j))
                        if j in SCAN_O:
                            scan_o(n - 3, other, SCAN_O.index(j))
                        if j == 13:
                            scan_sum(n - 3)
                    if prep:
                        if j == 4:
                            prep_rows(n - 1, other)
                        if j == 6:
                            prep_gram(n - 1, other)
                        if j == 9:
                            prep_turn_a(n - 1)
                        if j == 12:
                            prep_qk(n - 1, other)
                        if j == 13:
                            prep_turn_kv(n - 1, other, 1)
                        if j == 14:
                            prep_turn_kv(n - 1, other, 2)

            all_periods(pe, period)

            late_project()
            ffn(U_GU1, E_GU1, U_DOWN1, E_DOWN1, 3, 5, 11)

        @block.vector
        def _(dve):
            def gain_col(z, m):
                return prm[:, bass.ds(R_GAIN + 8 * z + m, 1)]

            def lo_of_x(count, lo, hi, xm, gain):
                dve.wait_ge(hi_ready, count)
                dve.scalar_tensor_tensor(out=lo, in0=xm, scalar=gain, in1=hi.bitcast(F32),
                                         op0=ALU.mult, op1=ALU.subtract).then_inc(lo_ready, 1)

            def fill_from_x(fill, z):
                for m in range(KT):
                    lo_of_x(8 * fill + m + 1, mov_lo[:, m, :], mov_hi[:, m, :], x[:, m, :],
                            gain_col(z, m))

            def fill_from(fill, n, src, k):
                dve.wait_ge(hi_ready, 8 * fill + n + 1)
                dve.tensor_tensor(mov_lo[:, k, :], src[:, k, :], mov_hi[:, k, :].bitcast(F32),
                                  ALU.subtract).then_inc(lo_ready, 1)

            dve.wait_ge(prm_loaded, 16)
            fill_from_x(0, 0)
            dve.tensor_scalar(nsink[:], prm[:, R_SINK:R_SINK + 8], -1.0, None,
                              ALU.mult).then_inc(nsink_ready, 1)
            for j in range(2):
                dve.memset(cx[:, j, 0:2], 0.0).then_inc(pad0, 1)

            dve.wait_ge(cst_loaded, 16)
            dve.wait_ge(rstd_ready, 1)
            dve.tensor_tensor(rstd2[:], rstd[:], rstd[:], ALU.mult).then_inc(rstd2_ready, 1)
            dve.wait_ge(rstd2_ready, 1)

            def head_gain(n):
                step(dve, hd_norm, n, "rsqrt")
                g = prm[:, R_QG:R_QG + 1] if n < 4 else prm[:, R_KG:R_KG + 1]
                dve.scalar_tensor_tensor(out=qk[:, n, :], in0=qk[:, n, :], scalar=g,
                                         in1=hrs[:, n % 2, :], op0=ALU.mult,
                                         op1=ALU.mult).then_inc(hd_gain, 1)

            def head_rope(n):
                dve.wait_ge(hd_rot, n + 1)
                step(dve, hd_rope, n - 1, "sum")
                dve.tensor_tensor(rope_s[:], bank[3][:], c_(C0_SIN, 0, T),
                                  ALU.mult).then_inc(hd_rope.sem, 1)
                dve.wait_ge(hd_cos, n + 1)
                step(dve, hd_rope, n, "sin")
                dve.tensor_tensor(qk[:, n, :], rope_c[:, n % 2, :], rope_s[:],
                                  ALU.add).then_inc(hd_rope.sem, 1)

            def take_conv(n):
                grp, r = divmod(n - 6, 6)
                kind, t = divmod(r, 2)
                c = 2 * grp + t
                dve.wait_ge(passes, n + 1)
                src = bank[n % 2][:]
                if kind == 0:
                    dve.tensor_tensor(gate_c[:, t, :], src, rstd2[:], ALU.mult).then_inc(taken, 1)
                elif kind == 1:
                    step(dve, cc_vec, c - 2, "tap2")
                    dve.wait_ge(pad0, 2)
                    dve.wait_ge(taken, n - 1)
                    dve.tensor_tensor(cx[:, t, 2:T + 2], src, gate_c[:, t, :],
                                      ALU.mult).then_inc(taken, 1)
                else:
                    dve.wait_ge(cc_scale, c + 1)
                    dve.tensor_tensor(mix[:, 4 + c, :], src, conv0[:, t, :],
                                      ALU.mult).then_inc(taken, 1)

            def conv_taps(c):
                dve.wait_ge(cc_tap, c + 1)
                t = c % 2
                for j in (1, 2):
                    if j == 2:
                        step(dve, cc_vec, c, "tap1")
                    dve.scalar_tensor_tensor(out=conv0[:, t, :], in0=cx[:, t, j:j + T],
                                             scalar=prm[:, R_CONV0 + 3 * c + j:R_CONV0 + 3 * c + j + 1],
                                             in1=conv0[:, t, :], op0=ALU.mult,
                                             op1=ALU.add).then_inc(cc_vec.sem, 1)

            def softmax_max(n):
                b, g = divmod(n, 2)
                r = n % 2
                cur = chunks(bank[5 + g][:])
                dve.wait_ge(scored, n + 1)
                mask = over_chunks(c_(C0_SUP).bitcast(U32))
                data = chunks(bank[4][:]) if b else c_(C0_NEG, 0, 1).unsqueeze(2).to_broadcast([P, 4, P])
                dve.copy_predicated(cur, mask, data).then_inc(sm_max.sem, 1)
                step(dve, sm_max, n, "join")
                dve.tensor_reduce(mx[:, r, :], cur, AX.X, ALU.max).then_inc(sm_max.sem, 1)
                step(dve, sm_max, n, "max")
                dve.wait_ge(nsink_ready, 1)
                dve.scalar_tensor_tensor(out=nmx[:, r, :], in0=mx[:, r, :], scalar=-(HEAD ** -0.5),
                                         in1=nsink[:, 4 * g:4 * g + 4], op0=ALU.mult,
                                         op1=ALU.min).then_inc(sm_max.sem, 1)
                step(dve, sm_max, n, "neg")
                dve.tensor_tensor(sgap[:, r, :], prm[:, R_SINK + 4 * g:R_SINK + 4 * g + 4], nmx[:, r, :],
                                  ALU.add).then_inc(sm_max.sem, 1)

            def softmax_den(n):
                r = n % 2
                step(dve, sm_exp, n, "sink")
                dve.tensor_tensor(den2[:, r, :], den[:, r, :], esink[:, r, :],
                                  ALU.add).then_inc(sm_den.sem, 1)
                step(dve, sm_den, n, "sum")
                dve.reciprocal(rden[:, r, :], den2[:, r, :]).then_inc(sm_den.sem, 1)

            def softmax_mask(n):
                r = n % 2
                dve.wait_ge(turned, n + 1)
                many(dve, pv_done, n - 1)
                pt = chunks(bank[7][:])
                dve.tensor_tensor(probT[:, r, 1], pt, over_chunks(upper[0]), ALU.mult).then_inc(sm_mask.sem, 1)
                dve.tensor_tensor(probT[:, r, 0], pt, over_chunks(lower[0]), ALU.mult).then_inc(sm_mask.sem, 1)

            for n in range(18):
                if 9 <= n <= 16:
                    softmax_den(n - 9)
                if n < 6:
                    dve.wait_ge(passes, n + 1)
                    dst = qk[:, n, :] if n < 5 else vT[:]
                    dve.tensor_tensor(dst, bank[n % 2][:], rstd[:], ALU.mult).then_inc(taken, 1)
                else:
                    take_conv(n)
                if 2 <= n <= 6:
                    head_gain(n - 2)
                if 3 <= n <= 7:
                    head_rope(n - 3)
                if 8 <= n < 16:
                    softmax_max(n - 8)
                if n in (8, 9, 14, 15):
                    conv_taps(n - 8 if n < 10 else n - 12)
                if 10 <= n:
                    softmax_mask(n - 10)
            for n, k in enumerate(MIX_ORDER):
                fill_from(1, n, mix, k)

            def residual(xm, src, npass):
                dve.wait_ge(passes, npass)
                dve.tensor_tensor(xm, src, xm, ALU.add).then_inc(taken, 1)

            def late_square(m):
                dve.wait_ge(squared, 8 * 3 + m + 1)
                dve.wait_ge(added.sem, 9 * 3 + 1 + m)
                dve.tensor_tensor(sqsum[:], sqsum[:], sq[:, m % 4, :], ALU.add).then_inc(added.sem, 1)

            def out_project(u0, z, fill):
                for m in range(KT):
                    residual(x[:, m, :], bank[m % 2][:], u0 + m + 1)
                fill_from_x(fill, z)

            def ffn(u_gu, e_gu, u_down, e_down, z, blk0, nz, fill):
                def block_(u0, blk, at, e_at):
                    for t in range(2):
                        dve.wait_ge(passes, u0 + t + 1)
                        many(dve, gated, 2 * blk + t - 1)
                        dve.tensor_tensor(gs[:, t, :], bank[t][:], rstd[:], ALU.mult).then_inc(taken, 1)
                    for t in range(2):
                        dve.wait_ge(passes, u0 + 3 + t)
                        many(dve, act_lo_ready, 2 * blk + t - 1)
                        dve.tensor_tensor(us[:, t, :], bank[2 + t][:], rstd[:], ALU.mult).then_inc(taken, 1)
                        dve.wait_ge(silu_g, 2 * blk + t + 1)
                        dve.wait_ge(taken, e_at + 3 + t)
                        dve.tensor_tensor(us[:, t, :], us[:, t, :], gs[:, t, :], ALU.mult).then_inc(gated, 1)
                    for t in range(2):
                        dve.wait_ge(act_hi_ready, 2 * blk + t + 1)
                        dve.wait_ge(gated, 2 * blk + t + 1)
                        dve.tensor_tensor(at(act_lo, t), us[:, t, :], at(act_hi, t).bitcast(F32),
                                          ALU.subtract).then_inc(act_lo_ready, 1)

                dve.wait_ge(rstd_ready, z + 1)
                block_(u_gu, blk0, lambda a, t: a[:, t, :], e_gu)
                with dve.Fori(0, 10) as i:
                    block_(u_gu + 4 + 4 * i, blk0 + 1 + i,
                           lambda a, t: a[:, bass.ds(2 * i + (2 + t), 1), :].rearrange("p a n -> p (a n)"),
                           e_gu + 4 + 4 * i)
                with dve.Fori(0, 4) as i:
                    for m in range(2):
                        at = bass.ds(2 * i + m, 1)
                        xm = x[:, at, :].rearrange("p a n -> p (a n)")
                        residual(xm, bank[m][:], u_down + 2 * m + 2 + 4 * i)
                        if nz is not None:
                            lo_of_x(8 * fill + m + 1 + 2 * i,
                                    mov_lo[:, at, :].rearrange("p a n -> p (a n)"),
                                    mov_hi[:, at, :].rearrange("p a n -> p (a n)"), xm,
                                    gain_col(nz, m + 2 * i))

            out_project(U_OUT0, 1, 2)
            ffn(U_GU0, E_GU0, U_DOWN0, E_DOWN0, 1, 0, 2, 3)

            def gate(ins):
                ins.then_inc(gt_vec.sem, 1)

            def after_gate(name):
                step(dve, gt_vec, 0, name)

            dve.wait_ge(passes, U_IN1)
            for k in range(KT):
                many(dve, gt_x_used, k - 1)
                dve.wait_ge(taken, E_IN1)
                dve.tensor_scalar((gam, gamL)[k % 2][:].rearrange("p c n -> p (c n)"), x[:, k, :],
                                  gain_col(2, k), None, ALU.mult).then_inc(gt_x, 1)
            for j in range(3):
                dve.memset(u[:, j, 0:3], 0.0).then_inc(zeroed, 1)
            dve.wait_ge(gt_x_used, KT)
            dve.wait_ge(rstd_ready, 3)
            gate(dve.tensor_tensor(ba, bank[6][0:16, :], rstd[0:16, :], ALU.mult))
            step(dve, gt_pe, 0, "turned")
            gate(dve.tensor_copy(flat(bt[:]), bank[5][:, 0:64]))
            gate(dve.tensor_copy(HP[:, :, 0:12],
                                 prm[:, R_HEAD:R_HEAD + 96].rearrange("p (h n) -> p h n", n=12)))
            step(dve, gt_act, 0, "ebeta")
            gate(dve.tensor_scalar(sm[:, 1], sm[:, 0], 1.0, None, ALU.add))
            after_gate("plus1")
            gate(dve.reciprocal(sm[:, 2], sm[:, 1]))
            after_gate("beta")
            by_head = sm[:, 2].rearrange("p c h -> p h c")
            gate(dve.tensor_copy(HP[:, :, H_BETA:H_BETA + NB], by_head))
            gate(dve.tensor_scalar(HP[:, :, H_NBETA:H_NBETA + NB], by_head, -1.0, None, ALU.mult))
            gate(dve.tensor_tensor(sm[:, 3], bt[:, :, 8:16], over_chunks(prm[:, R_DT:R_DT + 8]), ALU.add))
            after_gate("z")
            gate(dve.scalar_tensor_tensor(out=sm[:, 4], in0=sm[:, 3], scalar=-1.0, in1=sm[:, 3],
                                          op0=ALU.mult, op1=ALU.min))
            gate(dve.tensor_scalar(sm[:, 7], sm[:, 3], 0.0, None, ALU.max))
            step(dve, gt_act, 0, "log")
            after_gate("relu")
            gate(dve.tensor_tensor(sm[:, 1], sm[:, 7], sm[:, 5], ALU.add))
            after_gate("softplus")
            gate(dve.scalar_tensor_tensor(out=sm[:, 6], in0=sm[:, 1], scalar=-1.0,
                                          in1=over_chunks(esum[:]), op0=ALU.mult, op1=ALU.mult))
            after_gate("g")
            gate(dve.tensor_copy(HP[:, :, H_G:H_G + NB], sm[:, 6].rearrange("p c h -> p h c")))

            def gate_cumsum():
                step(dve, gt_pe, 0, "cum")
                gate(dve.tensor_copy(HP[:, :, H_GC:H_GC + NB],
                                     bank[6][:, 0:32].rearrange("p (c h) -> p h c", h=8)))
                after_gate("gc_h")

            def take(n, tile):
                dve.wait_ge(passes, U_IN1 + tile + 1 + 4 * n)
                src = bank[tile % 2][:]
                if tile < 3:
                    step(dve, taps, n - 1, ("q3", "k3", "v3")[tile])
                    if isinstance(n, int) and n == 0:
                        dve.wait_ge(zeroed, 3)
                    dst = u[:, tile, 3:T + 3]
                else:
                    dst = dno[:, bass.ds(n, 1), :].rearrange("p a n -> p (a n)")
                dve.tensor_tensor(dst, src, rstd[:], ALU.mult).then_inc(taken, 1)

            def conv_tap(n, par, part, j):
                if j == 1:
                    step(dve, tap0, n, "qkv"[part])
                else:
                    step(dve, taps, n, "qkv"[part] + str(j - 1))
                dve.scalar_tensor_tensor(out=qkv[:, par, part, :], in0=u[:, part, j:j + T],
                                         scalar=hp[:, par, H_TAP + 4 * part + j:H_TAP + 4 * part + j + 1],
                                         in1=qkv[:, par, part, :], op0=ALU.mult,
                                         op1=ALU.add).then_inc(taps.sem, 1)

            def prep(ins):
                ins.then_inc(pr_vec.sem, 1)

            def prep_norms(n, par):
                step(dve, pr_act, n, "rsk")
                prep(dve.tensor_tensor(qkv[:, par, 1, :], qkv[:, par, 1, :], nrs[:, 1, :], ALU.mult))
                prep(dve.scalar_tensor_tensor(out=qkv[:, par, 0, :], in0=qkv[:, par, 0, :],
                                              scalar=float(P) ** -0.5, in1=nrs[:, 0, :], op0=ALU.mult,
                                              op1=ALU.mult))

            def prep_gaps(n, par):
                step(dve, pr_pe, n, "rows")
                step(dve, pr_vec, n - 1, "kdec")
                step(dve, pr_pool, n - 1, "gamU")
                for c in range(NB):
                    prep(dve.tensor_scalar(gam[:, c, :], bank[4][:, c * P:(c + 1) * P],
                                           hp[:, par, H_GC + c:H_GC + c + 1], None, ALU.subtract))

            def prep_gap(n):
                step(dve, pr_vec, n, "d3")
                prep(dve.scalar_tensor_tensor(out=gam[:], in0=gam[:], scalar=-1.0, in1=gam[:],
                                              op0=ALU.mult, op1=ALU.min))

            def prep_a(n, par):
                step(dve, pr_pe, n, "gram")
                step(dve, pr_pool, n, "gamL")
                step(dve, pr_pe, n - 1, "turnA")
                for c in range(NB):
                    prep(dve.scalar_tensor_tensor(out=nA[:, c, :], in0=bank[5][:, c * P:(c + 1) * P],
                                                  scalar=hp[:, par, H_NBETA + c:H_NBETA + c + 1],
                                                  in1=gamL[:, c, :], op0=ALU.mult, op1=ALU.mult))

            def diag(lvl):
                return over_chunks(c_(C1_DIAG + P * (lvl - 1), 1), 2)

            def prep_att(n, par):
                step(dve, sc_pe, n - 2, "o3")
                step(dve, pr_pe, n, "qk")
                step(dve, pr_pool, n, "gamU")
                prep(dve.tensor_tensor(attT[:, par], chunks(bank[4][:]), gamU[:], ALU.mult))

            def prep_w(n, par):
                step(dve, pr_pe, n, "turnA")
                aT = bank[5][:].rearrange("p (q two n) -> p q two n", two=2, n=P)
                a = nA[:].rearrange("p (q two) n -> p q two n", two=2)
                prep(dve.tensor_tensor(W[:, par], aT[:, :, 0], a[:, :, 1], ALU.add))
                prep(dve.tensor_tensor(WT[:], aT[:, :, 1], a[:, :, 0], ALU.add))

            def prep_m(n, par):
                step(dve, pr_vec, n, "WT")
                prep(dve.tensor_tensor(M[:, par], WT[:], over_chunks(c_(C1_PAIR, 1), 2), ALU.mult))
                step(dve, pr_vec, n, "m")
                prep(dve.tensor_tensor(M[:, par], M[:, par], over_chunks(ident[1], 2), ALU.add))
                step(dve, pr_vec, n, "M")
                prep(dve.tensor_tensor(R[:, par], M[:, par], diag(1), ALU.mult))

            def prep_k(n, par):
                step(dve, pr_pe, n, "turnK")
                step(dve, pr_act, n, "gam")
                prep(dve.tensor_tensor(kdec[:, par], chunks(bank[5][:]),
                                       gam[:, :, P - 1:P].to_broadcast([P, NB, P]), ALU.mult))

            def prep_v(n, par):
                step(dve, pr_pe, n, "turnV")
                prep(dve.tensor_tensor(bv[:, par], chunks(bank[4][:]),
                                       along(hp[:, par, H_BETA:H_BETA + NB]), ALU.mult))
                prep(dve.tensor_copy(decb[:, par, :], chunks(eR[:])[:, :, P - 1]))
                prep(dve.tensor_copy(betab[:, par, :], hp[:, par, H_NBETA:H_NBETA + NB]))

            def inv(ins):
                ins.then_inc(iv_vec.sem, 1)

            def inv_y(n, par, lvl):
                step(dve, iv_pe, n, f"Y{lvl}")
                off = over_chunks(c_(C1_OFF + P * (lvl - 1), 1), 2)
                inv(dve.tensor_tensor(Y[:], pairs(bank[2][:, 0:2 * P]), off, ALU.mult))

            def xt(par, odd):
                return XT[:, par].rearrange("p (q two) n -> p q two n", two=2)[:, :, odd]

            def inv_x(n, par, lvl):
                step(dve, iv_pe, n, f"Z{lvl}")
                inv(dve.tensor_tensor(M[:, par], pairs(bank[2][:, 2 * P:]), M[:, par], ALU.add))
                step(dve, iv_vec, n, f"M{lvl}")
                if lvl < 6:
                    inv(dve.tensor_tensor(R[:, par], M[:, par], diag(lvl + 1), ALU.mult))
                else:
                    step(dve, sc_pe, n - 2, "o3")
                    inv(dve.tensor_tensor(xt(par, 1), M[:, par], over_chunks(upper[1], 2), ALU.mult))

            def inv_v(n, par, lvl):
                step(dve, iv_pe, n, f"T{lvl}")
                dst, mask = (V[:, par], diag(lvl + 1)) if lvl < 6 else (xt(par, 0), over_chunks(upper[1], 2))
                inv(dve.tensor_tensor(dst, pairs(bank[3][:, 0:2 * P]), mask, ALU.mult))

            def scan(ins):
                ins.then_inc(sc_vec.sem, 1)

            def scan_r(n, par, c):
                step(dve, sc_pe, n, f"k{c}")
                step(dve, sc_pe, n, f"v{c - 1}")
                step(dve, pr_vec, n, "beta")
                scan(dve.scalar_tensor_tensor(out=R1[:], in0=bank[6][:, 0:P],
                                              scalar=betab[:, par, c:c + 1], in1=bv[:, par, c, :],
                                              op0=ALU.mult, op1=ALU.add))

            def scan_vn(n, par, c):
                step(dve, sc_pe, n, f"v{c}")
                step(dve, sc_pe, n - 1 if c == 0 else n, "o3" if c == 0 else f"o{c - 1}")
                scan(dve.tensor_copy(vn[:], bank[6][:, P:2 * P]))

            def scan_s(n, par, c):
                step(dve, sc_pe, n, f"o{c}")
                if c == 0:
                    scan(dve.tensor_copy(S[:], bank[6][:, 2 * P:3 * P]))
                else:
                    scan(dve.scalar_tensor_tensor(out=S[:], in0=S[:], scalar=decb[:, par, c:c + 1],
                                                  in1=bank[6][:, 2 * P:3 * P], op0=ALU.mult,
                                                  op1=ALU.add))

            def scan_gain(n):
                step(dve, sc_act, n, "sq")
                dve.wait_ge(silu_z, n + 1)
                step(dve, sc_vec, n - 1, "out")
                z = dno[:, bass.ds(n, 1), :].rearrange("p a n -> p (a n)")
                scan(dve.scalar_tensor_tensor(out=og, in0=bank[7][:], scalar=prm[:, R_OG:R_OG + 1],
                                              in1=z, op0=ALU.mult, op1=ALU.mult))

            def scan_out(n):
                step(dve, sc_act, n, "rs")
                step(dve, sc_vec, n, "gain")
                z = dno[:, bass.ds(n, 1), :].rearrange("p a n -> p (a n)")
                scan(dve.tensor_tensor(z, og, ors[:], ALU.mult))

            def period(n, par, proj_, prep_, inv, scan_):
                other = 1 - par
                if isinstance(n, int) and n == 0:
                    take(0, 0)
                    gate_cumsum()
                if proj_:
                    step(dve, taps, n - 2, "v3")
                    step(dve, pr_vec, n - 2, "beta")
                    dve.tensor_copy(hp[:, par, :], HP[:, bass.ds(n, 1), :].rearrange("p a n -> p (a n)")
                                    ).then_inc(fetched, 1)
                for j in range(16):
                    if prep_ and j == 13:
                        prep_att(n - 1, other)
                    if not proj_ and (n, j) in EARLY_TAKEN:
                        m = EARLY_TAKEN[n, j]
                        residual(x[:, m, :], bank[m % 2][:], U_OUT1 + m + 1)
                    if inv:
                        if j in INV_Y:
                            inv_y(n - 2, par, INV_Y.index(j) + 1)
                        if j in INV_Z:
                            inv_x(n - 2, par, INV_Z.index(j) + 1)
                        if j in INV_T:
                            inv_v(n - 2, par, INV_T.index(j) + 1)
                    if scan_:
                        if j in SCAN_K:
                            scan_r(n - 3, other, SCAN_K.index(j) + 1)
                        if j in SCAN_V:
                            scan_vn(n - 3, other, SCAN_V.index(j))
                        if j in SCAN_O and j != SCAN_O[3]:
                            scan_s(n - 3, other, SCAN_O.index(j))
                        if j == 12:
                            scan_gain(n - 3)
                    if prep_:
                        if j == 3:
                            prep_norms(n - 1, other)
                        if j == 4:
                            prep_gaps(n - 1, other)
                        if j == 5:
                            prep_gap(n - 1)
                        if j == 7:
                            prep_a(n - 1, other)
                        if j == 10:
                            prep_w(n - 1, other)
                        if j == 11:
                            prep_m(n - 1, other)
                        if j == 14:
                            prep_k(n - 1, other)
                        if j == 15:
                            prep_v(n - 1, other)
                    if proj_ and j % 4 == 3 and not (isinstance(n, int) and n == 0 and j == 3):
                        take(n, j // 4)
                    if proj_ and j in TAPS:
                        conv_tap(n, par, *TAPS[j])
                if scan_:
                    scan_out(n - 3)
                if not proj_:
                    if n == 10:
                        residual(x[:, 7, :], bank[1][:], U_OUT1 + 8)
                    fill_from(4, n - 3, dno, n - 3)

            all_periods(dve, period)
            for m in range(KT):
                b, t = divmod(m, 2)
                if t == 0:
                    dve.wait_ge(late_half, b + 1)
                    dve.tensor_tensor(x[:, m, :], bank[t][:], x[:, m, :], ALU.add).then_inc(taken, 1)
                else:
                    residual(x[:, m, :], bank[t][:], U_LATE + b + 1)
                if 0 < m < KT - 1:
                    late_square(m - 1)
            for m in range(KT):
                if m == 5:
                    late_square(KT - 2)
                lo_of_x(8 * 5 + m + 1, mov_lo[:, m, :], mov_hi[:, m, :], x[:, m, :], gain_col(3, m))
            late_square(KT - 1)
            ffn(U_GU1, E_GU1, U_DOWN1, E_DOWN1, 3, 11, None, None)

        @block.scalar
        def _(act):
            def exp_table():
                act.preload_act_table_set("natural_log_exp_and_others")

            def silu_table():
                act.preload_act_table_set("silu_and_others")

            act.dma_start(prm[:], params).then_inc(prm_loaded, 16)
            act.dma_start(kpt[:], kept).then_inc(kept_loaded, 16)
            exp_table()

            def split(unit0, rounds=0):
                act.wait_ge(unit_loaded[unit0 % RING], 16 * (unit0 // RING + 1) + 16 * rounds)
                if not (isinstance(rounds, int) and unit0 + RING * rounds < 2):
                    act.wait_ge(passes, unit0 - 1 + RING * rounds)
                n = unit_tiles(unit0 + RING * rounds if isinstance(rounds, int) else unit0) * UW
                act.activation(w_hi[:, unit0 % 2, 0:n], raw[:, unit0 % RING, 0:n],
                               ACT.Copy).then_inc(w_hi_ready, 1)

            def round_x(hi, xm, gain):
                act.activation(hi, xm, ACT.Copy, scale=gain).then_inc(hi_ready, 1)

            def gain_col(z, m):
                return prm[:, bass.ds(R_GAIN + 8 * z + m, 1)]

            def fill_from(src, k):
                act.activation(mov_hi[:, k, :], src[:, k, :], ACT.Copy).then_inc(hi_ready, 1)

            def sq_free(z, m_abs, slots=4):
                many(act, added.sem, 9 * z + (m_abs if slots == 2 else max(m_abs - 2, 0)))

            def square_x(m, xm):
                act.activation(sq[:, m, :], xm, ACT.Square).then_inc(squared, 1)

            def rstd_of(z):
                act.wait_ge(norm_sum, z + 1)
                act.activation(rstd[:], bank[7][:], ACT.Ln, bias=eps_col,
                               scale=1.0 / D).then_inc(rstd_log, 1)
                act.wait_ge(rstd_log, z + 1)
                act.activation(rstd[:], rstd[:], ACT.Exp, scale=-0.5).then_inc(rstd_ready, 1)

            act.wait_ge(prm_loaded, 16)
            for m in range(KT):
                act.wait_ge(x_loaded[m // 2], 16)
                round_x(mov_hi[:, m, :], x[:, m, :], gain_col(0, m))
                if m == 0:
                    split(0)
                sq_free(0, m)
                square_x(m % 4, x[:, m, :])
                if m == 3:
                    act.dma_start(cst0[:], consts0).then_inc(cst_loaded, 16)
            split(1)
            act.wait_ge(kept_loaded, 16)
            rstd_of(0)

            def head_square(n):
                act.wait_ge(taken, n + 1)
                many(act, hd_sum, n - 1)
                act.activation(hsq[:, n % 2, :], qk[:, n, :], ACT.Square).then_inc(hd_sq, 1)

            def head_norm(n):
                act.wait_ge(hd_sum, n + 1)
                many(act, hd_gain, n - 1)
                act.activation(hrs[:, n % 2, :], bank[2][:], ACT.Ln, bias=eps_col,
                               scale=1.0 / HEAD).then_inc(hd_norm.sem, 1)
                step(act, hd_norm, n, "log")
                act.activation(hrs[:, n % 2, :], hrs[:, n % 2, :], ACT.Exp, scale=-0.5).then_inc(hd_norm.sem, 1)

            def first_tap(c):
                n = 8 + c if c < 2 else 12 + c
                act.wait_ge(taken, n + 1)
                many(act, taken, 10 + c - 2 + 1 if c > 1 else 0)
                act.activation(conv0[:, c % 2, :], cx[:, c % 2, 0:T], ACT.Copy,
                               scale=prm[:, R_CONV0 + 3 * c:R_CONV0 + 3 * c + 1]).then_inc(cc_tap, 1)

            def softmax_exp(n):
                g = n % 2
                r = n % 2
                step(act, sm_max, n, "neg")
                many(act, turned, n - 1)
                step(act, sm_den, n - 2, "sum")
                for t in range(4):
                    act.activation(prob[:, r, t, :], bank[5 + g][:, t * P:(t + 1) * P], ACT.Exp,
                                   bias=nmx[:, r, t:t + 1], scale=HEAD ** -0.5,
                                   accum_out=den[:, r, t:t + 1]).then_inc(sm_exp.sem, 1)
                step(act, sm_max, n, "gap")
                act.activation(esink[:, r, :], sgap[:, r, :], ACT.Exp).then_inc(sm_exp.sem, 1)

            for n in range(18):
                split(n + 2)
                if n < 5:
                    head_square(n)
                if 2 <= n <= 6:
                    head_norm(n - 2)
                if n in (8, 9, 14, 15):
                    first_tap(n - 8 if n < 10 else n - 12)
                if n == 7:
                    act.wait_ge(v_turned, 1)
                    act.activation(flat(vtok[:]), bank[7][:], ACT.Copy).then_inc(v_tok, 1)
                if 8 <= n < 16:
                    softmax_exp(n - 8)
                if n >= 12 and (n - 11) % 2 == 1:
                    b = (n - 12) // 2
                    act.wait_ge(pv_done, 2 * b + 2)
                    act.activation(mix[:, 0:4, b * P:(b + 1) * P], chunks(bank[2 + b % 2][:]),
                                   ACT.Copy).then_inc(y_copied, 1)
            act.wait_ge(passes, U_OUT0)
            act.wait_ge(taken, E_OUT0)
            for k in MIX_ORDER[0:4]:
                fill_from(mix, k)
            act.wait_ge(pv_done, 8)
            act.activation(mix[:, 0:4, 3 * P:4 * P], chunks(bank[3][:]), ACT.Copy).then_inc(y_copied, 1)
            act.wait_ge(y_copied, 4)
            for k in MIX_ORDER[4:8]:
                fill_from(mix, k)

            def next_input(z, e0, npass):
                act.wait_ge(passes, npass)
                for m in range(KT):
                    if m == KT - 1:
                        act.wait_ge(taken, e0 + KT)
                    round_x(mov_hi[:, m, :], x[:, m, :], gain_col(z, m))
                split(npass + 1)
                sq_free(z, KT - 1)
                square_x(3, x[:, KT - 1, :])
                split(npass + 2)
                rstd_of(z)

            def out_project(u0, e0, z):
                for m in range(KT):
                    if m < KT - 1:
                        split(u0 + m + 2)
                        act.wait_ge(taken, e0 + m + 1)
                        sq_free(z, m)
                        square_x(m % 4, x[:, m, :])
                next_input(z, e0, u0 + KT)

            def ffn(u_gu, e_gu, u_down, e_down, blk0, nz):
                def block_(unit0, rounds, blk, at, e_at, first=False):
                    for t in range(2):
                        if not first or t:
                            split(unit0 + t + 2, rounds)
                        act.wait_ge(taken, e_at + t + 1)
                        act.activation(gs[:, t, :], gs[:, t, :], ACT.Silu).then_inc(silu_g, 1)
                    for t in range(2):
                        split(unit0 + t + 4, rounds)
                        act.wait_ge(gated, 2 * blk + t + 1)
                        act.activation(at(t), us[:, t, :], ACT.Copy).then_inc(act_hi_ready, 1)

                def down_(unit0, rounds, at, e_at, m_at):
                    for m in range(2):
                        for half in range(2):
                            if unit0 + 2 * m + half + 2 < U_END:
                                split(unit0 + 2 * m + half + 2, rounds)
                        xm = x[:, at(m), :].rearrange("p a n -> p (a n)")
                        if nz is not None:
                            sq_free(nz, m_at + m, 2)
                        act.wait_ge(taken, e_at + m + 1)
                        if nz is None:
                            act.dma_start(outT[at(m), :, :].rearrange("a p n -> p (a n)"),
                                          xm).then_inc(out_done, 16)
                        else:
                            round_x(mov_hi[:, at(m), :].rearrange("p a n -> p (a n)"), xm,
                                    gain_col(nz, m_at + m))
                            square_x(m, xm)

                silu_table()
                block_(u_gu, 0, blk0, lambda t: act_hi[:, t, :], e_gu, first=True)
                with act.Fori(0, 9) as i:
                    block_(u_gu + 4, i, blk0 + 1 + i,
                           lambda t: act_hi[:, bass.ds(2 * i + (2 + t), 1), :].rearrange("p a n -> p (a n)"),
                           e_gu + 4 + 4 * i)
                block_(u_gu + 40, 0, blk0 + 10, lambda t: act_hi[:, 20 + t, :], e_gu + 40)
                with act.Fori(0, 3) as i:
                    down_(u_down, i, lambda m: bass.ds(2 * i + m, 1), e_down + 2 * i, 2 * i)
                down_(u_down + 12, 0, lambda m: bass.ds(6 + m, 1), e_down + 6, 6)
                if nz is not None:
                    exp_table()
                    rstd_of(nz)

            out_project(U_OUT0, E_OUT0, 1)
            ffn(U_GU0, E_GU0, U_DOWN0, E_DOWN0, 0, 2)
            act.wait_ge(passes, U_IN1)
            act.dma_start(cst1[:], consts1).then_inc(cst_loaded, 16)

            act.activation(esum[:], prm[:, R_ALOG:R_ALOG + 8], ACT.Exp).then_inc(gt_act.sem, 1)
            step(act, gt_vec, 0, "copied")
            act.activation(sm[:, 0], bt[:, :, 0:8], ACT.Exp, scale=-1.0).then_inc(gt_act.sem, 1)
            step(act, gt_vec, 0, "nabs")
            act.activation(sm[:, 5], sm[:, 4], ACT.Exp).then_inc(gt_act.sem, 1)
            step(act, gt_act, 0, "eabs")
            act.activation(sm[:, 5], sm[:, 5], ACT.Ln, bias=1.0).then_inc(gt_act.sem, 1)

            def first_tap1(n, par, part):
                act.wait_ge(fetched, n + 1)
                act.wait_ge(taken, E_IN1 + part + 1 + 4 * n)
                step(act, pr_pe, n - 2, "turnV")
                step(act, pr_pool, n - 2, "qd")
                act.activation(qkv[:, par, part, :], u[:, part, 0:T], ACT.Copy,
                               scale=hp[:, par, H_TAP + 4 * part:H_TAP + 4 * part + 1]
                               ).then_inc(tap0.sem, 1)

            def prep(ins):
                ins.then_inc(pr_act.sem, 1)

            def prep_squares(n, par):
                step(act, silu, n, "k")
                step(act, pr_vec, n - 1, "qn")
                for part in range(2):
                    for dst in (nsq, nsq_hi):
                        prep(act.activation(dst[:, part, :], qkv[:, par, part, :], ACT.Square))

            def prep_norms(n):
                for part, name in ((0, "q"), (1, "k")):
                    step(act, pr_pe, n, "sum" + name)
                    prep(act.activation(nrs[:, part, :], bank[5 - part][:], ACT.Ln, bias=eps_col))
                    step(act, pr_act, n, "ln" + name)
                    prep(act.activation(nrs[:, part, :], nrs[:, part, :], ACT.Exp, scale=-0.5))

            def prep_decays(n):
                step(act, pr_vec, n, "d3")
                step(act, pr_pool, n - 1, "qd")
                step(act, pr_vec, n - 1, "dec")
                prep(act.activation(eR[:], bank[4][:], ACT.Exp))
                step(act, pr_vec, n, "gap")
                prep(act.activation(flat(gam[:]), flat(gam[:]), ACT.Exp))

            def scan_square(n):
                step(act, sc_pe, n, "o3")
                step(act, sc_pe, n - 1, "sum")
                act.activation(osq, bank[7][:], ACT.Square).then_inc(sc_act.sem, 1)

            def scan_norm(n):
                step(act, sc_pe, n, "sum")
                step(act, sc_vec, n - 1, "out")
                act.activation(ors[:], bank[6][:], ACT.Ln, bias=eps_col,
                               scale=1.0 / P).then_inc(sc_act.sem, 1)
                step(act, sc_act, n, "log")
                act.activation(ors[:], ors[:], ACT.Exp, scale=-0.5).then_inc(sc_act.sem, 1)

            def silu_of_z(n):
                if not isinstance(n, int) or n >= 0:
                    act.wait_ge(taken, E_IN1 + 4 * n + 4)
                    z = dno[:, bass.ds(n, 1), :].rearrange("p a n -> p (a n)")
                    act.activation(z, z, ACT.Silu).then_inc(silu_z, 1)

            def period(n, par, proj_, prep_, inv, scan_):
                other = 1 - par
                if prep_:
                    prep_norms(n - 1)
                if proj_:
                    split(U_IN1 + 2, n)
                    first_tap1(n, par, 0)
                if not proj_ and n == DN_HEADS:
                    act.wait_ge(passes, U_OUT1)
                    for k in range(EARLY):
                        step(act, sc_vec, k, "out")
                        fill_from(dno, k)
                if prep_:
                    prep_decays(n - 1)
                if not proj_:
                    for m in EARLY_SPLITS[n][0]:
                        split(U_OUT1 + m + 2)
                if proj_:
                    split(U_IN1 + 3, n)
                    first_tap1(n, par, 1)
                if proj_:
                    split(U_IN1 + 4, n)
                    first_tap1(n, par, 2)
                if scan_:
                    scan_square(n - 3)
                    scan_norm(n - 3)
                if proj_ or prep_:
                    silu_table()
                    if proj_:
                        for part, name in enumerate("qkv"):
                            if name == "v":
                                silu_of_z(n - 1)
                            step(act, taps, n, name + "3")
                            act.activation(qkv[:, par, part, :], qkv[:, par, part, :],
                                           ACT.Silu).then_inc(silu.sem, 1)
                            if name == "k":
                                prep_squares(n, par)
                        split(U_IN1 + 5, n)
                    else:
                        silu_of_z(n - 1)
                    exp_table()
                if not proj_:
                    step(act, sc_vec, n - 3, "out")
                    fill_from(dno, n - 3)
                    for m in EARLY_SPLITS[n][1]:
                        split(U_OUT1 + m + 2)

            act.wait_ge(passes, U_IN1)
            act.activation(ones_r[:], ones, ACT.Copy).then_inc(ones_ready, 1)
            all_periods(act, period)
            for m in range(KT):
                if m % 2 == 0 and m < KT - 2:
                    split(U_LATE + m // 2 + 2)
                if m < KT - 1:
                    act.wait_ge(taken, E_LATE + m + 1)
                    sq_free(3, m)
                    square_x(m % 4, x[:, m, :])
            next_input(3, E_LATE, U_GU1)
            ffn(U_GU1, E_GU1, U_DOWN1, E_DOWN1, 11, None)
            act.wait_ge(out_done, 16 * KT)

        @block.gpsimd
        def _(pool):
            def add_squares(z):
                many(pool, norm_sum, z)
                pool.memset(sqsum[:], 0.0).then_inc(added.sem, 1)

            def add_square(z, slot, m_abs):
                pool.wait_ge(squared, 8 * z + m_abs + 1)
                pool.wait_ge(added.sem, 9 * z + 1 + m_abs)
                pool.tensor_tensor(sqsum[:], sqsum[:], sq[:, slot, :], ALU.add).then_inc(added.sem, 1)

            def split(unit0, rounds=0):
                pool.wait_ge(w_hi_ready, unit0 + 1 + RING * rounds)
                n = unit_tiles(unit0 + RING * rounds if isinstance(rounds, int) else unit0) * UW
                pool.tensor_tensor(w_lo[:, unit0 % 2, 0:n], raw[:, unit0 % RING, 0:n],
                                   w_hi[:, unit0 % 2, 0:n].bitcast(F32),
                                   ALU.subtract).then_inc(w_lo_ready, 1)

            split(0)
            add_squares(0)
            for m in range(KT):
                add_square(0, m % 4, m)
            split(1)

            def head_cos(n):
                pool.wait_ge(hd_gain, n + 1)
                step(pool, hd_rope, n - 2, "sum")
                pool.tensor_tensor(rope_c[:, n % 2, :], qk[:, n, :], c_(C0_COS, 0, T),
                                   ALU.mult).then_inc(hd_cos, 1)

            def conv_scale(c):
                step(pool, cc_vec, c, "tap2")
                pool.tensor_tensor(conv0[:, c % 2, :], conv0[:, c % 2, :], rstd[:],
                                   ALU.mult).then_inc(cc_scale, 1)

            def divide(n):
                r = n % 2
                step(pool, sm_den, n, "recip")
                pool.tensor_tensor(prob[:, r], prob[:, r], along(rden[:, r, :]), ALU.mult).then_inc(sm_div, 1)

            pool.wait_ge(cst_loaded, 16)
            for n in range(18):
                split(n + 2)
                if 2 <= n <= 6:
                    head_cos(n - 2)
                if 9 <= n <= 16:
                    divide(n - 9)
                if n in (8, 9, 14, 15):
                    conv_scale(n - 8 if n < 10 else n - 12)

            def out_project(u0, z):
                add_squares(z)
                for m in range(KT):
                    split(u0 + m + 2)
                    add_square(z, m % 4, m)

            def ffn(u_gu, u_down, nz):
                def down_(unit0, rounds, m_at):
                    for m in range(2):
                        for half in range(2):
                            if unit0 + 2 * m + half + 2 < U_END:
                                split(unit0 + 2 * m + half + 2, rounds)
                        if nz is not None:
                            add_square(nz, m, m_at + m)

                for t in range(4):
                    split(u_gu + t + 2)
                if nz is not None:
                    add_squares(nz)
                with pool.Fori(0, 9) as i:
                    for t in range(4):
                        split(u_gu + 4 + t + 2, i)
                for t in range(4):
                    split(u_gu + 40 + t + 2)
                with pool.Fori(0, 3) as i:
                    down_(u_down, i, 2 * i)
                down_(u_down + 12, 0, 6)

            out_project(U_OUT0, 1)
            ffn(U_GU0, U_DOWN0, 2)

            def prep(ins):
                ins.then_inc(pr_pool.sem, 1)

            def prep_los(n):
                for part, name in enumerate("qk"):
                    step(pool, pr_act, n, "hi" + name)
                    prep(pool.tensor_tensor(nsq_lo[:, part, :], nsq[:, part, :],
                                            nsq_hi[:, part, :].bitcast(F32), ALU.subtract))

            def prep_masks(n):
                step(pool, pr_act, n, "gam")
                step(pool, pr_vec, n - 1, "att")
                prep(pool.tensor_tensor(gamL[:], gam[:], over_chunks(lower[1]), ALU.mult))
                step(pool, pr_pool, n, "gamL")
                prep(pool.tensor_tensor(gamU[:], gam[:], over_chunks(upper[1]), ALU.mult))

            def prep_v(n, par):
                step(pool, pr_vec, n, "W")
                step(pool, iv_vec, n - 2, "XA")
                prep(pool.tensor_tensor(V[:, par], W[:, par], over_chunks(c_(C1_PAIR_V, 1), 2), ALU.mult))
                step(pool, pr_pool, n, "v")
                prep(pool.tensor_tensor(V[:, par], V[:, par], over_chunks(ident[1], 2), ALU.add))

            def prep_decayed(n, par):
                step(pool, pr_vec, n, "qn")
                step(pool, pr_act, n, "eR")
                step(pool, sc_pe, n - 2, "o3")
                prep(pool.tensor_tensor(kd[:, par, :], qkv[:, par, 1, :], eR[:], ALU.mult))
                prep(pool.tensor_tensor(qd[:, par, :], qkv[:, par, 0, :], eR[:], ALU.mult))

            def period(n, par, proj_, prep_, inv, scan_):
                other = 1 - par
                if proj_:
                    split(U_IN1 + 2, n)
                elif n == DN_HEADS:
                    for k in range(EARLY):
                        pool.wait_ge(hi_ready, 8 * 4 + k + 1)
                        pool.tensor_tensor(mov_lo[:, k, :], dno[:, k, :], mov_hi[:, k, :].bitcast(F32),
                                           ALU.subtract).then_inc(lo_ready, 1)
                if prep_:
                    prep_masks(n - 1)
                if proj_:
                    split(U_IN1 + 3, n)
                else:
                    for m in EARLY_SPLITS[n][0]:
                        split(U_OUT1 + m + 2)
                if prep_:
                    prep_v(n - 1, other)
                if proj_:
                    split(U_IN1 + 4, n)
                if prep_:
                    prep_decayed(n - 1, other)
                if proj_:
                    prep_los(n)
                    split(U_IN1 + 5, n)
                else:
                    for m in EARLY_SPLITS[n][1]:
                        split(U_OUT1 + m + 2)

            all_periods(pool, period)
            add_squares(3)
            for b in range(LATE_UNITS):
                split(U_LATE + b + 2)
            ffn(U_GU1, U_DOWN1, None)


def unit_tiles(unit):
    if U_OUT1 <= unit < U_GU1:
        return EARLY if unit < U_LATE else 2 * LATE
    return FH if U_DOWN0 <= unit < U_IN1 or U_DOWN1 <= unit else KT


MIX_ORDER = [4, 5, 6, 7, 0, 1, 2, 3]

INV_Y = (0, 2, 5, 7, 9, 11)
INV_Z = (1, 4, 6, 8, 10, 13)
INV_T = (2, 5, 7, 9, 11, 15)
SCAN_V = (0, 4, 7, 10)
SCAN_O = (1, 5, 8, 11)
SCAN_K = (3, 6, 9)
EARLY_PIECES = ((range(0, 2), ()), (range(2, 4), ()), (range(4, 5), range(0, 2)), ((), range(2, 5)))
EARLY_AT = ([(8, j) for j in range(7, 16)] + [(9, j) for j in range(0, 12)]
            + [(10, j) for j in (0, 1, 3, 4, 5, 7, 8, 9, 11, 14, 14)])
EARLY_STEPS = {at: [divmod(n, 4) for n, a in enumerate(EARLY_AT) if a == at] for at in EARLY_AT}
EARLY_TAKEN = {(EARLY_AT[4 * m + 4]): m for m in range(7)}
EARLY_SPLITS = {8: ((0,), (1,)), 9: ((2, 3, 4), ()), 10: ((5, 6), (7,))}

GATES_AT = (1, 5, 9)
TAPS = {5: (0, 1), 6: (0, 2), 7: (0, 3), 8: (1, 1), 9: (1, 2), 10: (1, 3), 12: (2, 1), 13: (2, 2), 14: (2, 3)}


def all_periods(eng, period):
    period(0, 0, True, False, False, False)
    period(1, 1, True, True, False, False)
    period(2, 0, True, True, True, False)
    period(3, 1, True, True, True, True)
    with eng.Fori(0, 2) as i:
        period(2 * i + 4, 0, True, True, True, True)
        period(2 * i + 5, 1, True, True, True, True)
    period(8, 0, False, True, True, True)
    period(9, 1, False, False, True, True)
    period(10, 0, False, False, False, True)


def constants():
    f = np.float32
    i = np.arange(P)
    kept = np.zeros((P, K_N), f)
    kept[:, K_ONES:K_ONES + P] = 1
    kept[:, K_EPS] = EPS
    c0 = np.zeros((P, C0_N), f)
    c1 = np.zeros((P, C1_N), f)
    for c in (c0, c1):
        c[:, C_ID:C_ID + P] = np.eye(P)
        c[:, C_UP:C_UP + P] = i[:, None] <= i[None]
        c[:, C_LOW:C_LOW + P] = i[:, None] > i[None]
    c0[:, C0_HALF:C0_HALF + P] = (i[:, None] // HEAD) == (i[None] // HEAD)
    for m in range(P):
        if m % HEAD < HEAD // 2:
            c0[m + HEAD // 2, C0_ROT + m] = -1
        else:
            c0[m - HEAD // 2, C0_ROT + m] = 1
    c0[:, C0_SUP:C0_SUP + P] = i[:, None] < i[None]
    inv_freq = f(10000.0) ** (-np.arange(0, HEAD, 2, dtype=f) / f(HEAD))
    ang = np.arange(T, dtype=f)[None] * inv_freq[i % (HEAD // 2)][:, None]
    c0[:, C0_COS:C0_COS + T] = np.cos(ang)
    c0[:, C0_SIN:C0_SIN + T] = np.sin(ang)
    c0[:, C0_NEG] = NEG
    row, col = i[:, None], i[None]
    c1[:, C1_PAIR:C1_PAIR + P] = row ^ 1 == col
    for lvl in range(1, 7):
        s = 1 << lvl
        even = row // s % 2 == 0
        same = row // s == col // s
        at = P * (lvl - 1)
        c1[:, C1_OFF + at:C1_OFF + at + P] = row // s ^ 1 == col // s
        c1[:, C1_DIAG + at:C1_DIAG + at + P] = same & np.where(even, row >= col, row <= col)
    c1[:, C1_PAIR_V:C1_PAIR_V + P] = c1[:, C1_PAIR:C1_PAIR + P] * c1[:, C1_DIAG:C1_DIAG + P]
    return kept, c0, c1


def units(w, kt):
    n = w.shape[1] // UW
    return np.ascontiguousarray(w.reshape(kt, P, n, UW).transpose(2, 1, 0, 3)).reshape(n, P, kt * UW)


def kernel(**inputs):
    import concourse.bacc as bacc
    from concourse.bass_utils import run_bass_kernel_spmd as run

    a = {k: np.asarray(v) for k, v in inputs.items()}
    cols = lambda v: v.reshape(-1, P).T
    rows = lambda v: np.broadcast_to(v.reshape(1, -1), (P, v.size))

    heads = [h for t in range(4) for h in (t, t + 4)]
    w = a["even_w_in"][0]
    w_q = w[:, 0:512].reshape(D, 8, HEAD)[:, heads].reshape(D, 512)
    w_kv = w[:, 512:768]
    gate_b, gate_c, xin = w[:, 768:1280], w[:, 1280:1792], w[:, 1792:2304]
    w_in0 = np.concatenate([w_q, w_kv] + [m[:, 2 * P * g:2 * P * (g + 1)] for g in range(2)
                                          for m in (gate_c, xin, gate_b)], 1)
    wo = a["even_w_out"][0]
    w_out0 = np.concatenate([wo[0:512].reshape(8, HEAD, D)[heads].reshape(512, D), wo[512:]], 0)
    w1, w_out1 = a["odd_w_in"][0], a["odd_w_out"][0]
    w_in1 = w1[:, 0:4 * D].reshape(D, 4, DN_HEADS, P).transpose(0, 2, 1, 3).reshape(D, 4 * D)

    def gate_up(m):
        g, u = (h.reshape(D, -1, 1, 2 * P) for h in (m[:, :FF], m[:, FF:]))
        return np.concatenate([g, u], 2).reshape(D, 2 * FF)

    def down(m):
        return np.ascontiguousarray(m.reshape(2, FH, P, KT, UW).transpose(3, 0, 2, 1, 4)
                                    ).reshape(DOWN_UNITS, P, FH * UW)

    params = np.concatenate([
        cols(a["even_norm"][0]), cols(a["ffn_norm"][0]), cols(a["odd_norm"][0]), cols(a["ffn_norm"][1]),
        np.tile(a["even_q_gain"][0], 2)[:, None], np.tile(a["even_k_gain"][0], 2)[:, None],
        rows(a["even_sinks"][0]),
        a["even_conv_w"][0].reshape(3, 4, P).transpose(2, 1, 0).reshape(P, 12),
        rows(a["odd_a_log"][0]), rows(a["odd_dt_bias"][0]), a["odd_o_gain"][0][:, None],
        a["odd_conv_w"][0].reshape(4, 3, DN_HEADS, P).transpose(3, 2, 1, 0).reshape(P, 96),
        w1[:, 4 * D:].reshape(KT, P, 16).transpose(1, 0, 2).reshape(P, 128),
    ], 1)
    kept, consts0, consts1 = constants()
    arrays = {
        "xT": a["x"][0].T.reshape(KT, P, T).transpose(1, 0, 2).reshape(P, KT * T),
        "params": params,
        "kept": kept, "consts0": consts0, "consts1": consts1,
        "w_in0": units(w_in0, KT), "w_out0": units(w_out0, KT),
        "w_gu0": units(gate_up(a["ffn_w_gate_up"][0]), KT), "w_down0": down(a["ffn_w_down"][0]),
        "w_in1": units(w_in1, KT), "w_early1": units(w_out1[:EARLY * P], EARLY),
        "w_late1": units(w_out1[EARLY * P:], LATE).reshape(LATE_UNITS, 2, P, -1).transpose(0, 2, 1, 3
                                                                          ).reshape(LATE_UNITS, P, -1),
        "w_gu1": units(gate_up(a["ffn_w_gate_up"][1]), KT), "w_down1": down(a["ffn_w_down"][1]),
    }
    nc = bacc.Bacc("TRN2", target_bir_lowering=False, num_devices=1)
    aps = []
    for name, v in arrays.items():
        arrays[name] = np.ascontiguousarray(v)
        aps.append(nc.dram_tensor(name, v.shape, F32, kind="ExternalInput").ap())
    outT = nc.dram_tensor("outT", (KT, P, T), F32, kind="ExternalOutput").ap()
    trunk(nc, *aps, outT)
    r = run(nc, [arrays], core_ids=[0])
    return np.ascontiguousarray(r.results[0]["outT"].reshape(D, T).T).reshape(1, T, D)
```
